# Optimizing a Trainium2 kernel written in Bass

```python
import math
import jax, jax.numpy as jnp
from jax import lax
import numpy as np

D_MODEL = 1024
BATCH = 1
SEQ = 512
DEPTH = 2
DEC_BATCH = 8
DEC_SEQ = 1
PAST_LEN = 2048
PAGE_SIZE = 128

N_MIXERS = 2
N_GMLP = (DEPTH + 1) // 2
N_ATT = DEPTH // 2

CHUNK = 128
GMLP_WIDTH = 2 * D_MODEL
GMLP_GROUPS = 8
GMLP_GROUP_DIM = GMLP_WIDTH // GMLP_GROUPS

N_HEADS = 16
HEAD_DIM = D_MODEL // N_HEADS
N_KV_HEADS = 4
GROUP = N_HEADS // N_KV_HEADS
IDX_HEADS = 8
IDX_DIM = 64
TOPK_MAX = 256
Q_BLOCK = 128
ROPE_THETA = 10000.0
IDX_SCALE = (IDX_DIM ** -0.5) * (IDX_HEADS ** -0.5)
ATT_SIZES = (N_HEADS * HEAD_DIM, N_KV_HEADS * HEAD_DIM, N_KV_HEADS * HEAD_DIM,
             IDX_HEADS * IDX_DIM, IDX_DIM, IDX_HEADS)
ATT_PROJ = sum(ATT_SIZES)

PEER_HEADS = 8
N_KEYS = 128
N_EXPERTS = N_KEYS * N_KEYS
PEER_TOPK = 16
PEER_KEY_DIM = 256
PEER_HALF = PEER_KEY_DIM // 2
PEER_BLOCK = 128

EPS = 1e-6

kernel_name = "gmlp_dsa_peer_hybrid_step"

def _rms(x, g):
    xf = x.astype(jnp.float32)
    y = xf * lax.rsqrt(jnp.mean(xf * xf, axis=-1, keepdims=True) + EPS)
    return (y * g.astype(jnp.float32)).astype(x.dtype)

def _rope(x, pos):
    half = x.shape[-1] // 2
    inv = jnp.exp(-math.log(ROPE_THETA) * jnp.arange(half, dtype=jnp.float32) / half)
    ang = pos.astype(jnp.float32)[:, None] * inv[None, :]
    cos = jnp.cos(ang)[:, None, :]
    sin = jnp.sin(ang)[:, None, :]
    xf = x.astype(jnp.float32)
    x1, x2 = xf[..., :half], xf[..., half:]
    return jnp.concatenate([x1 * cos - x2 * sin, x2 * cos + x1 * sin], axis=-1).astype(x.dtype)

def _gmlp_mix(h, w_in, v_g, w_s, b_s, w_out):
    B, T, _ = h.shape
    uv = h @ w_in
    u, v = uv[..., :GMLP_WIDTH], uv[..., GMLP_WIDTH:]
    v = _rms(v, v_g)
    n_chunks = -(-T // CHUNK)
    pad = n_chunks * CHUNK - T
    vp = jnp.pad(v, ((0, 0), (0, pad), (0, 0))).reshape(B, n_chunks, CHUNK, GMLP_GROUPS, GMLP_GROUP_DIM)
    causal = jnp.tril(jnp.ones((CHUNK, CHUNK), dtype=bool))
    ws = jnp.where(causal, w_s, 0)
    mixed = jnp.einsum('gts,bcsgd->bctgd', ws, vp) + b_s.T[None, None, :, :, None]
    mixed = mixed.reshape(B, n_chunks * CHUNK, GMLP_WIDTH)[:, :T]
    return (u * mixed) @ w_out, v

def _att_project(h, w_in, qn_g, kn_g, ikn_g, pos):
    B, T, _ = h.shape
    p = h @ w_in
    splits = [int(s) for s in np.cumsum(ATT_SIZES)[:-1]]
    q, k, v, qi, ki, wi = jnp.split(p, splits, axis=-1)
    q = _rope(_rms(q.reshape(B, T, N_HEADS, HEAD_DIM), qn_g), pos)
    k = _rope(_rms(k.reshape(B, T, N_KV_HEADS, HEAD_DIM), kn_g), pos)
    v = v.reshape(B, T, N_KV_HEADS, HEAD_DIM)
    qi = _rope(qi.reshape(B, T, IDX_HEADS, IDX_DIM), pos)
    ki = _rope(_rms(ki, ikn_g)[:, :, None, :], pos)[:, :, 0]
    return q, k, v, qi, ki, wi

def _sparse_attend(q, qi, wi, ki_all, q_pos, n_keep, gather_kv):
    B, Tq = q.shape[0], q.shape[1]
    s = jax.nn.relu(jnp.einsum('bthd,bsd->bths', qi, ki_all))
    score = jnp.einsum('bths,bth->bts', s, wi).astype(jnp.float32) * IDX_SCALE
    key_pos = jnp.arange(ki_all.shape[1])
    admissible = key_pos[None, :] <= q_pos[:, None]
    score = jnp.where(admissible[None], score, -jnp.inf)
    _, idx = lax.top_k(score, n_keep)
    sel_ok = idx <= q_pos[None, :, None]
    k_sel, v_sel = gather_kv(idx)
    qg = q.reshape(B, Tq, N_KV_HEADS, GROUP, HEAD_DIM)
    logits = jnp.einsum('bthgd,btnhd->bthgn', qg, k_sel).astype(jnp.float32) * (HEAD_DIM ** -0.5)
    logits = jnp.where(sel_ok[:, :, None, None, :], logits, -jnp.inf)
    prob = jax.nn.softmax(logits, axis=-1).astype(v_sel.dtype)
    o = jnp.einsum('bthgn,btnhd->bthgd', prob, v_sel)
    return o.reshape(B, Tq, N_HEADS * HEAD_DIM)

def _take_rows(a, idx):
    return jax.vmap(lambda ab, ib: ab[ib])(a, idx)

def _att_prompt(h, w_in, qn_g, kn_g, ikn_g, w_out):
    B, S, _ = h.shape
    pos = jnp.arange(S)
    q, k, v, qi, ki, wi = _att_project(h, w_in, qn_g, kn_g, ikn_g, pos)
    n_keep = min(TOPK_MAX, S // 4)
    nb = S // Q_BLOCK

    def gather(idx):
        return _take_rows(k, idx), _take_rows(v, idx)

    def blocks(a):
        return a.reshape((B, nb, Q_BLOCK) + a.shape[2:]).swapaxes(0, 1)

    def one_block(args):
        qb, qib, wib, posb = args
        return _sparse_attend(qb, qib, wib, ki, posb, n_keep, gather)

    o = lax.map(one_block, (blocks(q), blocks(qi), blocks(wi), pos.reshape(nb, Q_BLOCK)))
    o = o.swapaxes(0, 1).reshape(B, S, N_HEADS * HEAD_DIM)
    return o @ w_out, k, v, ki

def _att_sample(h, ck, cv, cik, page_table, w_in, qn_g, kn_g, ikn_g, w_out):
    B, T, _ = h.shape
    pos = PAST_LEN + jnp.arange(T)
    q, k, v, qi, ki, wi = _att_project(h, w_in, qn_g, kn_g, ikn_g, pos)
    n_pages = PAST_LEN // PAGE_SIZE
    ki_past = cik[page_table].reshape(B, n_pages * PAGE_SIZE, IDX_DIM)
    ki_all = jnp.concatenate([ki_past, ki], axis=1)
    n_keep = min(TOPK_MAX, (PAST_LEN + T) // 4)

    def gather(idx):
        is_new = (idx >= PAST_LEN)[..., None, None]
        past = jnp.minimum(idx, PAST_LEN - 1)
        phys = jnp.take_along_axis(page_table, (past // PAGE_SIZE).reshape(B, -1), axis=1).reshape(idx.shape)
        off = past % PAGE_SIZE
        new = jnp.clip(idx - PAST_LEN, 0, T - 1)
        k_sel = jnp.where(is_new, _take_rows(k, new), ck[phys, off])
        v_sel = jnp.where(is_new, _take_rows(v, new), cv[phys, off])
        return k_sel, v_sel

    o = _sparse_attend(q, qi, wi, ki_all, pos, n_keep, gather)
    return o @ w_out, k, v, ki

def _peer(h, w_q, sub_k1, sub_k2, expert_u, expert_v):
    shape = h.shape
    x = h.reshape(-1, D_MODEL)
    n = x.shape[0]
    nb = -(-n // PEER_BLOCK)
    xp = jnp.pad(x, ((0, nb * PEER_BLOCK - n), (0, 0))).reshape(nb, PEER_BLOCK, D_MODEL)

    def one_block(xb):
        q = (xb @ w_q).reshape(PEER_BLOCK, PEER_HEADS, 2, PEER_HALF)
        s1 = jnp.einsum('thd,kd->thk', q[:, :, 0], sub_k1).astype(jnp.float32)
        s2 = jnp.einsum('thd,kd->thk', q[:, :, 1], sub_k2).astype(jnp.float32)
        v1, i1 = lax.top_k(s1, PEER_TOPK)
        v2, i2 = lax.top_k(s2, PEER_TOPK)
        cand = (v1[..., :, None] + v2[..., None, :]).reshape(PEER_BLOCK, PEER_HEADS, PEER_TOPK * PEER_TOPK)
        cand_idx = (i1[..., :, None] * N_KEYS + i2[..., None, :]).reshape(PEER_BLOCK, PEER_HEADS, PEER_TOPK * PEER_TOPK)
        top_s, top_pos = lax.top_k(cand, PEER_TOPK)
        eidx = jnp.take_along_axis(cand_idx, top_pos, axis=-1)
        gate = jax.nn.softmax(top_s, axis=-1)
        u = expert_u[eidx]
        act = jax.nn.gelu(jnp.einsum('thkd,td->thk', u, xb))
        vv = expert_v[eidx]
        return jnp.einsum('thk,thkd->td', (gate * act).astype(vv.dtype), vv)

    y = lax.map(one_block, xp).reshape(-1, D_MODEL)[:n]
    return y.reshape(shape)

def setup_inputs(seed: int = 0) -> dict:
    key = jax.random.key(seed)
    ks = jax.random.split(key, 24)
    n_pages = PAST_LEN // PAGE_SIZE
    n_used = DEC_BATCH * n_pages
    n_pool = (5 * n_used + 3) // 4
    f32 = jnp.float32

    def nrm(k, shape, scale):
        return jax.random.normal(k, shape, f32) * scale

    def gain(k, shape):
        return 1.0 + 0.02 * jax.random.normal(k, shape, f32)

    page_table = jax.random.permutation(ks[0], n_pool)[:n_used].reshape(DEC_BATCH, n_pages).astype(jnp.int32)
    return {
        "x_prompt": nrm(ks[1], (BATCH, SEQ, D_MODEL), 1.0),
        "x_sample": nrm(ks[2], (DEC_BATCH, DEC_SEQ, D_MODEL), 1.0),
        "cache_k": nrm(ks[3], (N_ATT, n_pool, PAGE_SIZE, N_KV_HEADS, HEAD_DIM), 1.0),
        "cache_v": nrm(ks[4], (N_ATT, n_pool, PAGE_SIZE, N_KV_HEADS, HEAD_DIM), 1.0),
        "cache_idx_k": nrm(ks[5], (N_ATT, n_pool, PAGE_SIZE, IDX_DIM), 1.0),
        "page_table": page_table,
        "norm_mix_g": gain(ks[6], (DEPTH, D_MODEL)),
        "norm_ffn_g": gain(ks[7], (DEPTH, D_MODEL)),
        "gmlp_w_in": nrm(ks[8], (N_GMLP, D_MODEL, 2 * GMLP_WIDTH), D_MODEL ** -0.5),
        "gmlp_v_g": gain(ks[9], (N_GMLP, GMLP_WIDTH)),
        "gmlp_w_s": nrm(ks[10], (N_GMLP, GMLP_GROUPS, CHUNK, CHUNK), CHUNK ** -0.5),
        "gmlp_b_s": gain(ks[11], (N_GMLP, GMLP_GROUPS, CHUNK)),
        "gmlp_w_out": nrm(ks[12], (N_GMLP, GMLP_WIDTH, D_MODEL), 0.5 * GMLP_WIDTH ** -0.5),
        "att_w_in": nrm(ks[13], (N_ATT, D_MODEL, ATT_PROJ), D_MODEL ** -0.5),
        "att_q_norm_g": gain(ks[14], (N_ATT, HEAD_DIM)),
        "att_k_norm_g": gain(ks[15], (N_ATT, HEAD_DIM)),
        "att_idx_k_norm_g": gain(ks[16], (N_ATT, IDX_DIM)),
        "att_w_out": nrm(ks[17], (N_ATT, N_HEADS * HEAD_DIM, D_MODEL), (N_HEADS * HEAD_DIM) ** -0.5),
        "peer_w_q": nrm(ks[18], (DEPTH, D_MODEL, PEER_HEADS * PEER_KEY_DIM), D_MODEL ** -0.5),
        "peer_sub_k1": nrm(ks[19], (DEPTH, N_KEYS, PEER_HALF), PEER_HALF ** -0.5),
        "peer_sub_k2": nrm(ks[20], (DEPTH, N_KEYS, PEER_HALF), PEER_HALF ** -0.5),
        "peer_u": nrm(ks[21], (DEPTH, N_EXPERTS, D_MODEL), D_MODEL ** -0.5),
        "peer_v": nrm(ks[22], (DEPTH, N_EXPERTS, D_MODEL), 0.1),
    }

def reference(x_prompt, x_sample, cache_k, cache_v, cache_idx_k, page_table,
              norm_mix_g, norm_ffn_g,
              gmlp_w_in, gmlp_v_g, gmlp_w_s, gmlp_b_s, gmlp_w_out,
              att_w_in, att_q_norm_g, att_k_norm_g, att_idx_k_norm_g, att_w_out,
              peer_w_q, peer_sub_k1, peer_sub_k2, peer_u, peer_v):
    xp, xs = x_prompt, x_sample
    kp_l, vp_l, ip_l, ks_l, vs_l, is_l, cv_l = [], [], [], [], [], [], []
    for layer in range(DEPTH):
        a = layer // N_MIXERS
        hp = _rms(xp, norm_mix_g[layer])
        hs = _rms(xs, norm_mix_g[layer])
        if layer % N_MIXERS == 0:
            op, _ = _gmlp_mix(hp, gmlp_w_in[a], gmlp_v_g[a], gmlp_w_s[a], gmlp_b_s[a], gmlp_w_out[a])
            os_, v_rows = _gmlp_mix(hs, gmlp_w_in[a], gmlp_v_g[a], gmlp_w_s[a], gmlp_b_s[a], gmlp_w_out[a])
            cv_l.append(v_rows)
        else:
            op, kp, vp, ip = _att_prompt(hp, att_w_in[a], att_q_norm_g[a], att_k_norm_g[a],
                                         att_idx_k_norm_g[a], att_w_out[a])
            os_, ksm, vsm, ism = _att_sample(hs, cache_k[a], cache_v[a], cache_idx_k[a], page_table,
                                             att_w_in[a], att_q_norm_g[a], att_k_norm_g[a],
                                             att_idx_k_norm_g[a], att_w_out[a])
            kp_l.append(kp); vp_l.append(vp); ip_l.append(ip)
            ks_l.append(ksm); vs_l.append(vsm); is_l.append(ism)
        xp = xp + op
        xs = xs + os_
        xp = xp + _peer(_rms(xp, norm_ffn_g[layer]), peer_w_q[layer], peer_sub_k1[layer],
                        peer_sub_k2[layer], peer_u[layer], peer_v[layer])
        xs = xs + _peer(_rms(xs, norm_ffn_g[layer]), peer_w_q[layer], peer_sub_k1[layer],
                        peer_sub_k2[layer], peer_u[layer], peer_v[layer])
    new_k_prompt = jnp.stack(kp_l)
    new_v_prompt = jnp.stack(vp_l)
    new_idx_k_prompt = jnp.stack(ip_l)
    new_k_sample = jnp.stack(ks_l)
    new_v_sample = jnp.stack(vs_l)
    new_idx_k_sample = jnp.stack(is_l)
    new_chunk_v_sample = jnp.stack(cv_l)
    return (xp, xs, new_k_prompt, new_v_prompt, new_idx_k_prompt,
            new_k_sample, new_v_sample, new_idx_k_sample, new_chunk_v_sample)


_drawn_inputs = setup_inputs


def setup_inputs(seed=0):
    import zlib

    import numpy as np

    out = dict(_drawn_inputs(seed))
    spreads = {}
    factors = {'norm_ffn_g': 4.304,
     'gmlp_v_g': 2.776,
     'gmlp_b_s': 3.549,
     'att_q_norm_g': 8.0,
     'att_k_norm_g': 2.892}
    for name, (base, spread) in spreads.items():
        noise = np.random.default_rng([zlib.crc32(name.encode()), seed]).standard_normal(out[name].shape)
        drawn = base * np.exp(spread * noise) if base else spread * noise
        out[name] = __import__('jax').numpy.asarray(drawn.astype(out[name].dtype))
    for name, factor in factors.items():
        out[name] = (out[name] * factor).astype(out[name].dtype)
    return out
```

```python
import math
from contextlib import ExitStack

import numpy as np

import concourse.bass as bass
from concourse import mybir

F32 = mybir.dt.float32
F32R = mybir.dt.float32r
U32 = mybir.dt.uint32
I32 = mybir.dt.int32
ALU = mybir.AluOpType
ACT = mybir.ActivationFunctionType
AX = mybir.AxisListType.X

P = 128
D = 1024
KC = D // P
TP, TS = 512, 8
T = TP + TS
HT = T // 2
NB = 5
BLOCK = [(b * P, P) for b in range(4)] + [(TP, TS)]
EPS = 1e-6
WIDTH = 2 * D
VT = WIDTH // P
GROUPS = 8
NHEAD, NKV, HD, IH = 16, 4, 64, 8
PH, NK, TOPK = 8, 128, 16
HTN = 2 * PH
SLOTS = PH * TOPK
TG = 16
NG = (T + TG - 1) // TG
TW = NG * TG
GRP = 8
LOW = -3.0e38

PHASES = [("v_in", VT), ("u_in", VT), ("w_out", VT), ("q0", HTN), ("s0", NK), ("y0", NK),
          ("att", 20), ("ao", 8), ("q1", HTN), ("s1", NK), ("y1", NK)]
BASE = {}
N_SLABS = 0
for _name, _n in PHASES:
    BASE[_name] = N_SLABS
    N_SLABS += _n
LEN = dict(PHASES)
DVE_TILES = {}
_t = 0
for _name, _n in PHASES:
    DVE_TILES[_name] = _t
    _t += {"w_out": 8, "s0": 0, "s1": 0}.get(_name, _n)
ACT_TILES = {"s0": 0, "s1": NK}


class Count:

    def __init__(self):
        self.at = 0

    def up(self, by=1):
        self.at = self.at + by
        return by


OUTS = {"yT": (P, KC, T), "chunk_v": (TS, WIDTH), "kT": (HD, NKV, T), "vT": (P, 2, T), "kiT": (HD, T)}

TILES = [("ki", 0), ("wi", 0)] + [("qi", j) for j in range(4)] + [("k", j) for j in range(NKV)] + [
    ("v", j) for j in range(2)] + [("q", j) for j in range(8)]
NORMED = {"ki": 2, "k": 1, "q": 0}
ROPED = {"ki", "k", "q", "qi"}
PAST, PAGES, NPOOL = 2048, 16, 160
SK = PAST + 1
UNIT = 4
NU = PAGES // UNIT
UK = UNIT * P
IDX_SCALE = (HD ** -0.5) * (IH ** -0.5)
KEEP_P, KEEP_S = 128, 256
OUT = -1.0e30


def build(nc, a, outs, layers=2):
    LAST_L = layers - 1
    stop_slab = N_SLABS if layers == 2 else BASE["att"]
    es = ExitStack()
    with es:
        def sem(name):
            return es.enter_context(nc.semaphore(name))

        START = 16512

        def at(name, shape, dt, offset):
            assert offset + int(np.prod(shape[1:])) * 4 <= 212800, (name, offset)
            return nc.alloc_sbuf_tensor_at(name, shape, dt, offset=START + offset)

        place = [0]

        def sb(name, shape, dt=F32):
            t = at(name, shape, dt, place[0])
            place[0] += (int(np.prod(shape[1:])) * 4 + 31) // 32 * 32
            return t

        x = sb("x", [P, KC, T])
        h_at = place[0]
        h_hi = sb("h_hi", [P, KC, T], F32R)
        h_lo = sb("h_lo", [P, KC, T], F32R)
        g_hi = at("g_hi", [P, VT, T], F32R, h_at)
        raw = [sb(f"raw{r}", [P, KC, P]) for r in range(4)]
        w_hi = [sb(f"w_hi{r}", [P, KC, P], F32R) for r in range(2)]
        w_lo = [sb(f"w_lo{r}", [P, KC, P], F32R) for r in range(2)]
        ident = sb("ident", [P, P])
        ones = sb("ones", [P, P])
        gains = sb("gains", [P, 4, KC])
        iota = sb("iota", [P, P])
        subk = sb("subk", [P, 4, P])
        ms = sb("ms", [P, T])
        rms = sb("rms", [P, T])
        rstd = sb("rstd", [P, T])
        top = place[0]

        def region(start=None):
            p = [top if start is None else start]

            def take(name, shape, dt=F32):
                t = at(name, shape, dt, p[0])
                p[0] += (int(np.prod(shape[1:])) * 4 + 31) // 32 * 32
                take.end = p[0]
                return t
            take.end = p[0]
            return take

        take = region()
        u_at = take.end
        u = take("u", [P, VT, T])
        g_lo = at("g_lo", [P, VT, T], F32R, u_at)
        sq_at = take.end
        sq = take("sq", [P, KC, T])
        junk = at("junk", [P, WIDTH], F32, sq_at)
        vtok = take("vtok", [P, NB, WIDTH])
        vT = take("vT", [P, 2, T])
        vgain = take("vgain", [P, WIDTH])
        mbias = take("mbias", [P, GROUPS, P])
        wsT = take("wsT", [P, GROUPS, P])
        wdiag = take("wdiag", [TS, GROUPS, TS])
        vss = take("vss", [P, NB])
        vms = take("vms", [P, NB])
        vrms = take("vrms", [P, NB])
        vrstd = take("vrstd", [P, NB])
        mixb = take("mixb", [P, 2, T])
        wcaus = take("wcaus", [P, P])
        weye = take("weye", [TS, TS])
        end_g = take.end

        take = region()
        qT = take("qT", [P, HTN, T])
        gelu = take("gelu", [P, 2, T])
        sc_at = take.end
        sc = take("sc", [P, HTN, P])
        work_at = take.end
        work = take("work", [P, HTN, P])
        cand = at("cand", [P, PH, TOPK, TOPK], F32, sc_at)
        cwork = at("cwork", [P, PH, TOPK * TOPK], F32, work_at)
        hot = at("hot", [P, PH, TOPK, TOPK], F32, work_at)
        keyv = take("keyv", [P, HTN, TOPK])
        keyi = take("keyi", [P, HTN, TOPK], U32)
        keyf = take("keyf", [P, HTN, TOPK])
        topv = take("topv", [P, PH, TOPK])
        topd = take("topd", [P, PH, TOPK])
        topp = take("topp", [P, PH, TOPK], U32)
        row = take("row", [P, 2, PH, TOPK], U32)
        rowf = take("rowf", [P, 2, PH, TOPK])
        route = take("route", [P, 3, PH, TOPK])
        gsum = take("gsum", [P, 2, PH])
        idxT = take("idxT", [P, 2, T])
        gateT = take("gateT", [P, T])
        gate_hi = take("gate_hi", [P, T], F32R)
        gate_lo = gateT
        HG = TG // 2
        hot1 = [take(f"hot1_{r}", [P, HG, P], F32R) for r in range(2)]
        hot2 = [take(f"hot2_{r}", [P, HG, P]) for r in range(2)]
        hg_hi = [take(f"hg_hi{r}", [P, HG, P], F32R) for r in range(2)]
        hg_lo = [take(f"hg_lo{r}", [P, HG, P], F32R) for r in range(2)]
        gout = [take(f"gout{r}", [P, P, TG]) for r in range(2)]
        end_s = take.end

        take = region()
        abuf = [take(f"abuf{r}", [P, GRP, TW]) for r in range(2)]
        gbuf = [take(f"gbuf{r}", [P, NG, GRP, TG]) for r in range(2)]
        y_hi = [h_hi, take("y_hi1", [P, GRP, T], F32R)]
        y_lo = [h_lo, take("y_lo1", [P, GRP, T], F32R)]
        end_y = take.end

        take = region()
        kiT = take("kiT", [P, T])
        wiT = take("wiT", [P, T])
        qi_at = take.end
        qiT = take("qiT", [P, 4, T])
        score8 = at("score8", [TS, SK], F32, qi_at)
        kT2 = take("kT2", [P, NKV, T])
        vA = take("vA", [P, 2, T])
        v_tok = take("v_tok", [P, NB, 2 * P])
        qA = take("qA", [P, 8, T])
        wi_tok = take("wi_tok", [P, 4, IH])
        mx = take("mx", [P, 64])
        nmx = take("nmx", [P, 64])
        psums = take("psums", [P, 64])
        rinv = take("rinv", [P, 64])
        m8 = take("m8", [P, 3, 8])
        qiM = take("qiM", [HD, TS * (HD + 8)])
        assert take.end >= sq_at + 4 * KC * T
        t_at = take.end
        cosT = take("cosT", [P, T])
        sinT = take("sinT", [P, T])
        rot = take("rot", [P, P])
        headones = take("headones", [P, P])
        traw = [take(f"traw{r}", [P, T]) for r in range(2)]
        sqh = [take(f"sqh{r}", [P, T]) for r in range(2)]
        ra = take("ra", [P, T])
        rb = take("rb", [P, T])
        ms_h = take("ms_h", [P, T])
        rms_h = take("rms_h", [P, T])
        after_tiles = take.end
        again_take = region(t_at)
        prob = [again_take(f"prob{r}", [P, 512]) for r in range(2)]
        probT = [again_take(f"probT{r}", [P, 4, P]) for r in range(2)]
        o_tok = again_take("o_tok", [P, D])
        pT_s = again_take("pT_s", [P, PAGES, P])
        assert again_take.end <= after_tiles
        relu = prob
        idxs = take("idxs", [P, 4, 512])
        cbias = take("cbias", [P, P])
        again = take("again", [P, 3])
        sel8 = take("sel8", [8, HD])
        e64 = take("e64", [HD, TS])
        e8 = take("e8", [P, TS])
        e8T = take("e8T", [TS, P])
        wiB = take("wiB", [HD, TS])
        knew = take("knew", [P, 2, TS])
        pnew = take("pnew", [P, TS])
        pnewT = take("pnewT", [TS, P])
        oS = take("oS", [P, 8, TS])
        smx = take("smx", [P, 4])
        table = take("table", [1, TS * PAGES], I32)
        unit = [take(f"unit{r}", [P, 2, UK]) for r in range(4)]
        qM = take("qM", [P, 2, TS * (P + 16)])
        logits_at = take.end
        logits = take("logits", [P, SK])
        relu_s = at("relu_s", [HD, SK], F32, logits_at)
        end_a = take.end


        acc = es.enter_context(nc.psum_tensor("acc", [P, 2, 2, 512], F32))
        misc = es.enter_context(nc.psum_tensor("misc", [P, 4, 512], F32))

        act_d = [nc.dram_tensor(f"act_d{l}", [NK, P, T], F32).ap() for l in range(2)]
        gate_d = [nc.dram_tensor(f"gate_d{l}", [NG, P, NK, TG], F32).ap() for l in range(2)]

        raw_loaded = [sem(f"raw_loaded{r}") for r in range(4)]
        hi_done, lo_done, slab_done = sem("hi_done"), sem("lo_done"), sem("slab_done")
        acc_free_dve, acc_free_act = sem("acc_free_dve"), sem("acc_free_act")
        loaded = sem("loaded")
        sq_done, sumsq_done, ms_done = sem("sq_done"), sem("sumsq_done"), sem("ms_done")
        rms_done, rstd_done, hf_done = sem("rms_done"), sem("rstd_done"), sem("hf_done")
        h_hi_done, h_lo_done = sem("h_hi_done"), sem("h_lo_done")
        vT_done, vtr_done, vtok_done = sem("vT_done"), sem("vtr_done"), sem("vtok_done")
        vss_done, vms_done, vrms_done = sem("vss_done"), sem("vms_done"), sem("vrms_done")
        vrstd_done, vnorm_done = sem("vrstd_done"), sem("vnorm_done")
        mix_done, mix_added, g_done = sem("mix_done"), sem("mix_added"), sem("g_done")
        g_hi_done, g_lo_done = sem("g_hi_done"), sem("g_lo_done")
        u_done, x_done, qT_done = sem("u_done"), sem("x_done"), sem("qT_done")
        subk_loaded = sem("subk_loaded")
        score_done, score_taken = sem("score_done"), sem("score_taken")
        dve_step, act_step = sem("dve_step"), sem("act_step")
        gate_exp_in, gate_exp_done = sem("gate_exp_in"), sem("gate_exp_done")
        route_done, routeT_done = sem("route_done"), sem("routeT_done")
        slotT_done, gate_lo_done = sem("slotT_done"), sem("gate_lo_done")
        hot2_done, hot_done, hg_lo_done, gate_mm = sem("hot2_done"), sem("hot_done"), sem("hg_lo_done"), sem("gate_mm")
        gate_taken = sem("gate_taken")
        gate_stored = [sem(f"gate_stored{r}") for r in range(2)]
        gelu_done = sem("gelu_done")
        act_stored = [sem(f"act_stored{r}") for r in range(2)]
        group_loaded = [sem(f"group_loaded{r}") for r in range(2)]
        y_mult, y_hi_done, y_lo_done = sem("y_mult"), sem("y_hi_done"), sem("y_lo_done")
        pad_done = sem("pad_done")
        stored = sem("stored")
        att_loaded, sqh_done, traw_done = sem("att_loaded"), sem("sqh_done"), sem("traw_done")
        hs_done, hs_taken, rot_done = sem("hs_done"), sem("hs_taken"), sem("rot_done")
        rms_h_done, rope_done = sem("rms_h_done"), sem("rope_done")
        qM_ready, sel_ready = sem("qM_ready"), sem("sel_ready")
        prep_done, prep_taken = sem("prep_done"), sem("prep_taken")
        idx_done, relu_done, idx_added = sem("idx_done"), sem("relu_done"), sem("idx_added")
        unit_loaded = [sem(f"unit_loaded{r}") for r in range(4)]
        unit_used = sem("unit_used")
        s_idx_done, s_relu_done = sem("s_idx_done"), sem("s_relu_done")
        s_score_done, s_score_taken = sem("s_score_done"), sem("s_score_taken")
        s_log_done, s_log_taken = sem("s_log_done"), sem("s_log_taken")
        log_done, log_taken, nmx_done = sem("log_done"), sem("log_taken"), sem("nmx_done")
        exp_done, ptr_done, pT_done, pv_done = sem("exp_done"), sem("ptr_done"), sem("pT_done"), sem("pv_done")
        o_done, oT_done, oT_hi, oT_lo = sem("o_done"), sem("oT_done"), sem("oT_hi"), sem("oT_lo")
        mask_ready, bias_done, bias_taken = sem("mask_ready"), sem("bias_done"), sem("bias_taken")
        s_top = sem("s_top")
        s_max_done, s_exp_done, s_prob_done = sem("s_max_done"), sem("s_exp_done"), sem("s_prob_done")
        s_ptr_done, s_pT_done = sem("s_ptr_done"), sem("s_pT_done")
        s_pv_done, oS_done = sem("s_pv_done"), sem("oS_done")
        kv_out = sem("kv_out")
        vout = sem("vout")

        block = es.enter_context(nc.Block())

        N_CONST = 11
        N_ATT = 11

        @block.sync
        def _(sp):
            def load(n, r):
                sp.dma_start(raw[r][:], a["slabs"][n].rearrange("p (c m) -> p c m", c=KC)).then_inc(
                    raw_loaded[r], 16)

            sp.dma_start(x[:], a["xT"]).then_inc(loaded, 16)
            for r in range(4):
                load(r, r)
            def loads(first, last):
                with sp.Fori(first // 4, last // 4, 1) as q:
                    for r in range(4):
                        sp.wait_ge(hi_done, q * 4 + (r - 3))
                        sp.wait_ge(lo_done, q * 4 + (r - 3))
                        load(q * 4 + r, r)

            def page(b, u, j):
                return sp.value_load(table[0:1, bass.ds(b * PAGES + u * UNIT + j, 1)], min_val=0, max_val=NPOOL - 1)

            loads(4, min(stop_slab, BASE["ao"] + 4))
            if layers == 2:
                sp.wait_ge(att_loaded, 16 * N_ATT)
                with sp.Fori(0, NU, 1) as u:
                    for b in range(TS):
                        r = b % 4
                        sp.wait_ge(unit_used, u * TS + (b + 1))
                        for j in range(UNIT):
                            sp.dma_start(unit[r][0:HD, 0, j * P:(j + 1) * P],
                                         a["cikT"][bass.ds(page(b, u, j), 1)].squeeze(0)).then_inc(unit_loaded[r], 16)
                with sp.Fori(0, NU, 1) as u:
                    for b in range(TS):
                        r = b % 4
                        sp.wait_ge(unit_used, u * TS + (NU * TS + b + 1))
                        for j in range(UNIT):
                            sp.dma_start(unit[r][:, :, j * P:(j + 1) * P],
                                         a["ckT"][bass.ds(page(b, u, j), 1)].squeeze(0)).then_inc(unit_loaded[r], 16)
                with sp.Fori(0, TS, 1) as b:
                    for u in range(NU):
                        sp.wait_ge(unit_used, b * NU + (2 * NU * TS + u + 1))
                        for j in range(UNIT):
                            sp.dma_start(unit[u][:].rearrange("p a (b f) -> p (a b) f", f=2 * P)[:, j, :],
                                         a["cv"][bass.ds(page(b, u, j), 1)].squeeze(0)).then_inc(unit_loaded[u], 16)
                loads(BASE["ao"] + 4, N_SLABS)

        @block.tensor
        def _(pe):
            def slab(n, r, par, m_hi, m_lo, start=True, stop=True, free=None):
                pe.wait_ge(hi_done, n + 1)
                pe.wait_ge(lo_done, n + 1)
                if free is not None:
                    pe.wait_ge(*free)
                for c in range(KC):
                    for w, m in ((w_hi[r], m_hi), (w_hi[r], m_lo), (w_lo[r], m_hi)):
                        for half in range(2):
                            last = pe.matmul(acc[:, par, half, 0:HT], w[:, c, :],
                                             m(c)[:, half * HT:(half + 1) * HT],
                                             start=start and c == 0 and w is w_hi[r] and m is m_hi,
                                             stop=stop and c == KC - 1 and w is w_lo[r])
                last.then_inc(slab_done, 1)

            def norm(k):
                for c in range(KC):
                    pe.wait_ge(sq_done, k * KC + c + 1)
                    for half in range(2):
                        last = pe.matmul(misc[:, half, 0:HT], ones[:], sq[:, c, half * HT:(half + 1) * HT],
                                         start=c == 0, stop=c == KC - 1)
                last.then_inc(sumsq_done, 1)
                pe.wait_ge(h_lo_done, (k + 1) * KC)

            hh = lambda c: h_hi[:, c, :]
            hl = lambda c: h_lo[:, c, :]

            pe.wait_ge(loaded, 16 * N_CONST)
            norm(0)

            def turn_v_tile(n, par):
                for b, (t0, w) in enumerate(BLOCK):
                    last = pe.transpose(misc[0:w, 2 * par + b // 4, (b % 4) * P:(b % 4 + 1) * P],
                                        vT[:, par, t0:t0 + w], ident[:])
                last.then_inc(vtr_done, 1)

            def v_steps(n, first):
                for r in range(4):
                    slab(n + r, r % 2, r % 2, hh, hl, free=(acc_free_dve, n + r + 1))
                    if not (first and r == 0):
                        m = n + r - 1
                        pe.wait_ge(acc_free_dve, m + 3)
                        if not first or r >= 3:
                            pe.wait_ge(vtok_done, m - 1)
                        turn_v_tile(m, (r + 1) % 2)

            v_steps(0, True)
            with pe.Fori(4, VT, 4) as n:
                v_steps(n, False)
            pe.wait_ge(acc_free_dve, VT + 2)
            pe.wait_ge(vtok_done, VT - 2)
            turn_v_tile(VT - 1, 1)

            def mix(f):
                par = f % 2
                g = f // (VT // GROUPS)
                if f == 0:
                    pe.wait_ge(vnorm_done, NB)
                if f >= 2:
                    pe.wait_ge(mix_added, 2 * (f - 1))
                for b, (t0, w) in enumerate(BLOCK):
                    rhs = wsT[:, g, :] if b < 4 else wdiag[:, g, :]
                    last = pe.matmul(misc[:, 2 * par + b // 4, (b % 4) * P:(b % 4) * P + w],
                                     vtok[0:w, b, f * P:(f + 1) * P], rhs, start=True, stop=True)
                last.then_inc(mix_done, 1)

            for f in range(VT):
                n = BASE["u_in"] + f
                slab(n, n % 2, n % 2, hh, hl, free=(acc_free_dve, DVE_TILES["u_in"] + f + 1))
                if f >= 4:
                    mix(f - 4)
            for f in range(VT - 4, VT):
                mix(f)

            pe.wait_ge(g_lo_done, VT)
            with pe.Fori(0, 8, 2) as m:
                for par in range(2):
                    for kh in range(2):
                        slab(m * 2 + (BASE["w_out"] + 2 * par + kh), kh, par,
                             lambda c: g_hi[:, kh * KC + c, :], lambda c: g_lo[:, kh * KC + c, :],
                             start=kh == 0, stop=kh == 1,
                             free=(acc_free_dve, m + (DVE_TILES["w_out"] + par + 1)) if kh == 0 else None)

            def linear(phase):
                with pe.Fori(0, LEN[phase], 4) as i:
                    for r in range(4):
                        slab(i + (BASE[phase] + r), r % 2, r % 2, hh, hl,
                             free=(acc_free_dve, i + (DVE_TILES[phase] + r + 1)))

            def peer(l):
                base = BASE[f"s{l}"]
                done = [0]

                def s_slab(i, k):
                    slab(i + (base + k), k % 2, k % 2, hh, hl, free=(acc_free_act, i + (ACT_TILES[f"s{l}"] + k + 1)))

                def s_only(count):
                    with pe.Fori(done[0], done[0] + count, 2) as i:
                        s_slab(i, 0)
                        s_slab(i, 1)
                    done[0] += count

                def gates(half, par, width):
                    pe.wait_ge(hot_done, half + 1)
                    pe.wait_ge(hg_lo_done, half + 1)
                    for q in range(2):
                        pe.wait_ge(gate_taken, half * 2 + q + 1)
                        for j in range(4):
                            t = q * 4 + j
                            for part in (hg_hi, hg_lo):
                                last = pe.matmul(misc[:, q, j * P:(j + 1) * P], hot1[par][:, t, :],
                                                 part[par][:, t, :], start=part is hg_hi, stop=part is hg_lo)
                        last.then_inc(gate_mm, 1)

                H0 = l * (2 * NG - 1)
                pe.wait_ge(acc_free_dve, DVE_TILES[f"q{l}"] + HTN + 2)
                pe.wait_ge(subk_loaded, 16 * (l + 1))
                for b, (t0, w) in enumerate(BLOCK):
                    B = l * NB + b
                    if b:
                        pe.wait_ge(gate_taken, 2 * (H0 + b * P // HG) + 2)
                        pe.wait_ge(slotT_done, B)
                    for j in range(4):
                        for k in range(4):
                            ht = 4 * j + k
                            last = pe.matmul(misc[0:w, j, k * P:(k + 1) * P], qT[:, ht, t0:t0 + w],
                                             subk[:, 2 * l + ht % 2, :], start=True, stop=True)
                        last.then_inc(score_done, 1)
                    s_only(16)
                    pe.wait_ge(route_done, B + 1)
                    pe.wait_ge(score_taken, 4 * (B + 1))
                    for k in range(3):
                        last = pe.transpose(misc[:, 2, k * P:k * P + w],
                                            route[0:w, k].rearrange("p h k -> p (h k)"), ident[0:w, 0:w])
                    last.then_inc(routeT_done, 1)
                    if b < 4:
                        with pe.Fori(0, 8, 2) as i:
                            for r in range(2):
                                s_slab(i, done[0] + r)
                                for q in range(2):
                                    gates(i * 2 + (H0 + b * P // HG + 2 * r + q), q, HG)
                        done[0] += 8
                    else:
                        gates(H0 + TP // HG, 0, HG)
                s_only(NK - done[0])

                base = BASE[f"y{l}"]
                W0 = l * NK

                def y_group(j, par):
                    for c in range(GRP):
                        m_hi = lambda k: y_hi[par][:, k, :]
                        m_lo = lambda k: y_lo[par][:, k, :]
                        if c == 0:
                            pe.wait_ge(y_lo_done, j * GRP + (W0 + GRP))
                        slab(j * GRP + (base + c), c % 2, c % 2, m_hi, m_lo,
                             free=(acc_free_dve, j * GRP + (DVE_TILES[f"y{l}"] + c + 1)))

                with pe.Fori(0, NK // GRP, 2) as j:
                    y_group(j, 0)
                    y_group(j + 1, 1)

            def attention():
                base = BASE["att"]
                norm_at = [0]
                n_rot = [0]
                D0 = DVE_TILES["att"]

                def after(s):
                    kind, j = TILES[s]
                    par = s % 2
                    if kind not in ROPED:
                        return
                    pe.wait_ge(traw_done, n_rot[0] + 1)
                    if kind in NORMED:
                        pe.wait_ge(sqh_done, norm_at[0] + 1)
                        pe.wait_ge(hs_taken, norm_at[0])
                        for half in range(2):
                            last = pe.matmul(misc[:, half, 0:HT], headones[:], sqh[par][:, half * HT:(half + 1) * HT],
                                             start=True, stop=True)
                        last.then_inc(hs_done, 1)
                        norm_at[0] += 1
                    for half in range(2):
                        last = pe.matmul(acc[:, par, half, 0:HT], rot[:], traw[par][:, half * HT:(half + 1) * HT],
                                         start=True, stop=True)
                    last.then_inc(rot_done, 1)
                    n_rot[0] += 1

                pe.wait_ge(att_loaded, 16 * N_ATT)
                for s in range(20):
                    slab(base + s, s % 2, s % 2, hh, hl, free=(acc_free_dve, D0 + s + 1))
                    if s:
                        after(s - 1)
                after(19)

                pe.wait_ge(rope_done, 20)
                pe.wait_ge(sel_ready, 1)
                for b in range(4):
                    pe.transpose(misc[:, 2, b * IH:(b + 1) * IH], wiT[0:IH, b * P:(b + 1) * P], ident[0:IH, 0:IH])
                pe.matmul(misc[0:HD, 3, 0:TS], sel8[:], wiT[0:IH, TP:T], start=True, stop=True).then_inc(prep_done, 1)
                for j in range(2):
                    for b, (t0, w) in enumerate(BLOCK):
                        bank = misc[0:w, j, b * P:(b + 1) * P] if b < 4 else acc[0:w, 0, 0, j * P:(j + 1) * P]
                        last = pe.transpose(bank, vA[:, j, t0:t0 + w], ident[:])
                last.then_inc(prep_done, 1)

                pe.wait_ge(prep_taken, 2)
                for i in range(3 * IH):
                    b, h = 1 + i // IH, i % IH
                    p0 = (h % 2) * HD
                    if i >= 2:
                        pe.wait_ge(relu_done, i - 1)
                    pe.matmul(misc[:, 2 + i % 2, 0:(b + 1) * P], qiT[p0:p0 + HD, h // 2, b * P:(b + 1) * P],
                              kiT[p0:p0 + HD, 0:(b + 1) * P], start=True, stop=True).then_inc(idx_done, 1)

                pe.wait_ge(relu_done, 3 * IH)
                pe.wait_ge(qM_ready, 1)
                for u in range(NU):
                    if u >= 2:
                        pe.wait_ge(s_relu_done, u - 1)
                    for b in range(TS):
                        r = b % 4
                        pe.wait_ge(unit_loaded[r], 16 * UNIT * (2 * u + b // 4 + 1))
                        last = pe.matmul(misc[0:HD, 2 + u % 2, :], qiM[:, b * HD:(b + 1) * HD], unit[r][0:HD, 0, :],
                                         start=b == 0, stop=b == TS - 1)
                        last.then_inc(unit_used, 1)
                pe.wait_ge(s_relu_done, NU - 1)
                for b in range(TS):
                    last = pe.matmul(misc[0:HD, 2, 0:1], qiM[:, b * HD:(b + 1) * HD], kiT[0:HD, TP + b:TP + b + 1],
                                     start=b == 0, stop=b == TS - 1)
                last.then_inc(s_idx_done, 1)
                for u in range(NU + 1):
                    n = UK if u < NU else 1
                    pe.wait_ge(s_relu_done, NU + 1)
                    if u >= 2:
                        pe.wait_ge(s_score_taken, u - 1)
                    pe.matmul(misc[0:TS, 2 + u % 2, 0:n], wiB[:], relu_s[:, u * UK:u * UK + n], start=True,
                              stop=True).then_inc(s_score_done, 1)

                pe.wait_ge(s_score_taken, NU + 1)
                for u in range(NU):
                    if u >= 2:
                        pe.wait_ge(s_log_taken, u - 1)
                    for b in range(TS):
                        r = b % 4
                        pe.wait_ge(unit_loaded[r], 16 * UNIT * (2 * (NU + u) + b // 4 + 1))
                        for p in range(2):
                            last = pe.matmul(misc[:, 2 + u % 2, :], qM[:, p, b * P:(b + 1) * P], unit[r][:, p, :],
                                             start=b == 0 and p == 0, stop=b == TS - 1 and p == 1)
                        last.then_inc(unit_used, 1)
                pe.wait_ge(s_log_taken, NU - 1)
                for b in range(TS):
                    for p in range(2):
                        last = pe.matmul(misc[:, 2, 0:1], qM[:, p, b * P:(b + 1) * P], knew[:, p, b:b + 1],
                                         start=b == 0 and p == 0, stop=b == TS - 1 and p == 1)
                last.then_inc(s_log_done, 1)

                def log_of(i):
                    b, h = divmod(i, NHEAD)
                    p0 = (h % 2) * HD
                    if i >= 2:
                        pe.wait_ge(log_taken, i - 1)
                    pe.matmul(acc[:, 0, i % 2, 0:(b + 1) * P], qA[p0:p0 + HD, h // 2, b * P:(b + 1) * P],
                              kT2[p0:p0 + HD, h // 4, 0:(b + 1) * P], start=True, stop=True).then_inc(log_done, 1)

                def turn(i):
                    b, h = divmod(i, NHEAD)
                    pe.wait_ge(exp_done, i + 1)
                    if i >= 2:
                        pe.wait_ge(pT_done, i - 1)
                    if h < 2 and b:
                        pe.wait_ge(oT_lo, 2 * b)
                    for k in range(b + 1):
                        last = pe.transpose(acc[:, 1, i % 2, k * P:(k + 1) * P], prob[i % 2][:, k * P:(k + 1) * P],
                                            ident[:])
                    last.then_inc(ptr_done, 1)

                def pv(i):
                    b, h = divmod(i, NHEAD)
                    pe.wait_ge(pT_done, i + 1)
                    if i >= 2:
                        pe.wait_ge(o_done, i - 1)
                    for k in range(b + 1):
                        last = pe.matmul(misc[:, i % 2, 0:HD], probT[i % 2][:, k, :],
                                         v_tok[:, k, (h // 4) * HD:(h // 4 + 1) * HD], start=k == 0, stop=k == b)
                    last.then_inc(pv_done, 1)

                for b in range(4):
                    for h in range(NHEAD + 2):
                        i = b * NHEAD + h
                        if h < NHEAD:
                            log_of(i)
                        if 1 <= h <= NHEAD:
                            turn(i - 1)
                        if h >= 2:
                            pv(i - 2)
                    pe.wait_ge(o_done, NHEAD * (b + 1))
                    pe.wait_ge(pT_done, NHEAD * (b + 1))
                    for k in range(8):
                        last = pe.transpose(acc[:, 1, k // 4, (k % 4) * P:(k % 4 + 1) * P], o_tok[:, k * P:(k + 1) * P],
                                            ident[:])
                        if k % 4 == 3:
                            last.then_inc(oT_done, 1)

                pe.wait_ge(mask_ready, 1)
                for u in range(NU + 1):
                    n = UK if u < NU else 1
                    if u >= 2:
                        pe.wait_ge(bias_taken, u - 1)
                    pe.matmul(misc[:, 2 + u % 2, 0:n], e8T[:], score8[:, u * UK:u * UK + n], start=True,
                              stop=True).then_inc(bias_done, 1)
                pe.wait_ge(s_prob_done, 2)
                for k in range(NU):
                    if k >= 2:
                        pe.wait_ge(s_pT_done, k - 1)
                    for j in range(UNIT):
                        g = k * UNIT + j
                        last = pe.transpose(misc[:, 2 + k % 2, j * P:(j + 1) * P], logits[:, g * P:(g + 1) * P], ident[:])
                    last.then_inc(s_ptr_done, 1)
                pe.wait_ge(s_pT_done, NU - 1)
                pe.transpose(misc[0:TS, 2, 0:P], pnew[:], ident[:]).then_inc(s_ptr_done, 1)
                pe.wait_ge(s_pT_done, NU + 1)
                pe.wait_ge(oT_lo, 8)
                for b in range(TS):
                    for u in range(NU):
                        pe.wait_ge(unit_loaded[u], 16 * UNIT * (4 * NU + b + 1))
                        vals = unit[u][:].rearrange("p a (b f) -> p (a b) f", f=2 * P)
                        for j in range(UNIT):
                            for p in range(2):
                                c0 = b * 16 + p * 8
                                last = pe.matmul(misc[:, p, b * 8:b * 8 + 8], vals[:, j, p * P:(p + 1) * P],
                                                 pT_s[:, u * UNIT + j, c0:c0 + 8], start=u == 0 and j == 0, stop=False)
                        last.then_inc(unit_used, 1)
                    for p in range(2):
                        c0 = b * 16 + p * 8
                        last = pe.matmul(misc[:, p, b * 8:b * 8 + 8], v_tok[0:TS, 4, p * P:(p + 1) * P],
                                         pnewT[:, c0:c0 + 8], start=False, stop=True)
                last.then_inc(s_pv_done, 1)
                pe.wait_ge(oS_done, 2)

            norm(1)
            linear("q0")
            peer(0)
            if layers == 2:
                norm(2)
                attention()
                linear("ao")
                norm(3)
                linear("q1")
                peer(1)

        @block.scalar
        def _(act):
            step = Count()

            def split(q, r, first=False):
                act.wait_ge(raw_loaded[r], q * 16 + 16)
                if not first:
                    act.wait_ge(slab_done, q * 4 + (r - 1))
                act.activation(w_hi[r % 2][:], raw[r][:], ACT.Copy).then_inc(hi_done, 1)

            def ahead(q, r, last=False):
                if not last:
                    split(q + 1 if r == 3 else q, (r + 1) % 4)

            def norm(k, x_ready):
                for c in range(KC):
                    if x_ready is not None:
                        act.wait_ge(*x_ready(c))
                    act.activation(sq[:, c, :], x[:, c, :], ACT.Square).then_inc(sq_done, 1)
                act.wait_ge(ms_done, k + 1)
                act.activation(rms[:], ms[:], ACT.Sqrt).then_inc(rms_done, 1)
                for c in range(KC):
                    act.wait_ge(hf_done, k * KC + c + 1)
                    act.activation(h_hi[:, c, :], sq[:, c, :], ACT.Copy).then_inc(h_hi_done, 1)

            act.dma_start(ident[:], a["ident"]).then_inc(loaded, 16)
            act.dma_start(ones[:], a["ones"]).then_inc(loaded, 16)
            act.dma_start(gains[:], a["gains"]).then_inc(loaded, 16)
            act.dma_start(iota[:], a["iota"]).then_inc(loaded, 16)
            act.dma_start(vgain[:], a["vgain"].partition_broadcast(P)).then_inc(loaded, 16)
            act.dma_start(mbias[:].rearrange("p g t -> p (g t)"), a["mbias"].partition_broadcast(P)).then_inc(loaded, 16)
            act.dma_start(wsT[:], a["wsT"]).then_inc(loaded, 16)
            act.dma_start(wdiag[:], a["wdiag"]).then_inc(loaded, 16)
            act.dma_start(subk[:, 0:2, :], a["subk"][:, 0:2, :]).then_inc(subk_loaded, 16)
            act.dma_start(subk[:, 2:4, :], a["subk"][:, 2:4, :]).then_inc(subk_loaded, 16)
            act.dma_start(wcaus[:], a["wcaus"]).then_inc(loaded, 16)
            act.dma_start(weye[:], a["weye"]).then_inc(loaded, 16)

            split(0, 0, first=True)
            act.wait_ge(loaded, 16 * N_CONST)
            norm(0, None)

            def v_steps(q, first):
                for r in range(4):
                    ahead(q, r)
                    if not (first and r == 0):
                        m = q * 4 + (r - 1)
                        par = (r + 1) % 2
                        act.wait_ge(vtr_done, m + 1)
                        act.activation(vtok_tile(m, 0, 4), misc[:, 2 * par, :].rearrange("p (b f) -> p b f", b=4),
                                       ACT.Copy)
                        act.activation(vtok_tile(m, 4, 5), misc[0:TS, 2 * par + 1, 0:P].unsqueeze(1),
                                       ACT.Copy).then_inc(vtok_done, 1)

            def vtok_tile(m, b0, b1):
                f = m * P if isinstance(m, int) else m * P
                t = vtok[:, b0:b1, bass.ds(f, P)]
                return t if b0 == 0 else vtok[0:TS, b0:b1, bass.ds(f, P)]

            v_steps(0, True)
            with act.Fori(1, VT // 4, 1) as q:
                v_steps(q, False)
            act.wait_ge(vtr_done, VT)
            act.activation(vtok_tile(VT - 1, 0, 4), misc[:, 2, :].rearrange("p (b f) -> p b f", b=4), ACT.Copy)
            act.activation(vtok_tile(VT - 1, 4, 5), misc[0:TS, 3, 0:P].unsqueeze(1), ACT.Copy).then_inc(vtok_done, 1)

            act.wait_ge(vtok_done, VT)
            for b, (t0, w) in enumerate(BLOCK):
                if b:
                    act.wait_ge(vss_done, b)
                act.activation(junk[0:w, :], vtok[0:w, b, :], ACT.Square, accum_out=vss[0:w, b:b + 1]).then_inc(
                    vss_done, 1)
            act.wait_ge(vms_done, 2)
            act.activation(vrms[:, 0:4], vms[:, 0:4], ACT.Sqrt).then_inc(vrms_done, 1)
            act.activation(vrms[0:TS, 4:5], vms[0:TS, 4:5], ACT.Sqrt).then_inc(vrms_done, 1)

            for f in range(VT):
                n = BASE["u_in"] + f
                ahead(n // 4, n % 4)
            for f in range(VT):
                if f == 0:
                    act.wait_ge(vnorm_done, NB)
                    act.dma_start(outs["chunk_v"], vtok[0:TS, 4, :]).then_inc(vout, 16)
                    act.wait_ge(slab_done, BASE["w_out"])
                act.wait_ge(g_done, f + 1)
                act.activation(g_hi[:, f, :], u[:, f, :], ACT.Copy).then_inc(g_hi_done, 1)

            def plain(phase, last=False):
                q0 = BASE[phase] // 4
                with act.Fori(q0, q0 + LEN[phase] // 4, 1) as q:
                    for r in range(4):
                        ahead(q, r)

            plain("w_out")
            norm(1, lambda c: (acc_free_dve, DVE_TILES["w_out"] + c + 3))
            plain("q0")

            def peer(l):
                q0 = BASE[f"s{l}"] // 4
                B0 = BASE[f"s{l}"]
                done = [0]
                H0 = l * (2 * NG - 1)

                def s_step(q, r):
                    ahead(q + q0, r)
                    n = q * 4 + r
                    par = r % 2
                    act.wait_ge(slab_done, n + (B0 + 1))
                    act.wait_ge(act_stored[par], (q * 2 + (l * NK // 2 + r // 2)) * 16)
                    act.activation(gelu[:, par, :].rearrange("p (h t) -> p h t", h=2), acc[:, par, :, 0:HT],
                                   ACT.Gelu_apprx_tanh).then_inc(acc_free_act, 1)
                    act.wait_ge(acc_free_act, n + (l * NK + 3))
                    act.dma_start(act_d[l][n], gelu[:, par, :]).then_inc(act_stored[par], 16)

                def s_only(count):
                    with act.Fori(done[0] // 4, (done[0] + count) // 4, 1) as q:
                        for r in range(4):
                            s_step(q, r)
                    done[0] += count

                def take_gates(half, cpar, hpar, w=HG):
                    for q in range(2):
                        act.wait_ge(gate_mm, half * 2 + q + 1)
                        t0 = hpar * HG + q * 4
                        act.activation(gout[cpar][:, :, t0:t0 + 4].rearrange("p i t -> p t i"),
                                       misc[:, q, :].rearrange("p (t i) -> p t i", t=4),
                                       ACT.Copy).then_inc(gate_taken, 1)

                def store_gates(chunk, cpar, taken):
                    act.wait_ge(gate_taken, taken)
                    act.dma_start(gate_d[l][chunk], gout[cpar][:]).then_inc(gate_stored[cpar], 16)

                for b, (t0, w) in enumerate(BLOCK):
                    B = l * NB + b
                    for j in range(4):
                        act.wait_ge(score_done, 4 * B + j + 1)
                        act.activation(sc[0:w, 4 * j:4 * j + 4, :].rearrange("p k i -> p (k i)"),
                                       misc[0:w, j, :], ACT.Copy).then_inc(score_taken, 1)
                    s_only(8)
                    act.wait_ge(gate_exp_in, B + 1)
                    act.activation(route[0:w, 2], topd[0:w], ACT.Exp).then_inc(gate_exp_done, 1)
                    s_only(8)
                    act.wait_ge(routeT_done, B + 1)
                    act.activation(idxT[:, :, t0:t0 + w], misc[:, 2, 0:2 * P].rearrange("p (k t) -> p k t", k=2)[:, :, 0:w],
                                   ACT.Copy).then_inc(act_step, step.up())
                    act.activation(gateT[:, t0:t0 + w], misc[:, 2, 2 * P:2 * P + w], ACT.Copy).then_inc(
                        act_step, step.up())
                    act.wait_ge(act_step, step.at)
                    act.activation(gate_hi[:, t0:t0 + w], gateT[:, t0:t0 + w], ACT.Copy).then_inc(slotT_done, 1)
                    if b < 4:
                        C0 = b * P // TG
                        with act.Fori(done[0] // 4, done[0] // 4 + 2, 1) as q:
                            for r in range(4):
                                s_step(q, r)
                                chunk = q * 4 + (r + C0 - done[0])
                                act.wait_ge(gate_stored[r % 2],
                                            (q * 2 + (C0 - done[0]) // 2 + r // 2 + l * ((NG + 1 - 0) // 2 if r % 2 == 0 else NG // 2)) * 16)
                                take_gates(chunk * 2 + H0, r % 2, 0)
                                take_gates(chunk * 2 + (H0 + 1), r % 2, 1)
                                store_gates(chunk, r % 2, chunk * 4 + (2 * H0 + 4 + 2))
                        done[0] += 8
                    else:
                        act.wait_ge(gate_stored[0], (NG // 2 + l * ((NG + 1) // 2)) * 16)
                        take_gates(H0 + TP // HG, 0, 0)
                        store_gates(NG - 1, 0, 2 * (H0 + TP // HG) + 2 + 2)
                s_only(NK - done[0])

                J = NK // GRP
                W0 = l * NK

                def load_group(j, par):
                    act.dma_start(abuf[par][:, :, 0:T], act_d[l][bass.ds(j * GRP, GRP)].rearrange("i p t -> p i t")).then_inc(
                        group_loaded[par], 16)
                    act.dma_start(gbuf[par][:], gate_d[l][:, :, bass.ds(j * GRP, GRP), :].rearrange(
                        "n p i t -> p n i t")).then_inc(group_loaded[par], 16)

                def hi_part(j, c, par):
                    act.wait_ge(y_mult, j * GRP + (W0 + c + 1))
                    act.activation(y_hi[par][:, c, :], abuf[par][:, c, 0:T], ACT.Copy).then_inc(y_hi_done, 1)

                for par in range(2):
                    act.wait_ge(act_stored[par], (l + 1) * (NK // 2) * 16)
                act.wait_ge(gate_stored[0], (l + 1) * ((NG + 1) // 2) * 16)
                act.wait_ge(gate_stored[1], (l + 1) * (NG // 2) * 16)
                act.wait_ge(pad_done, l + 1)
                load_group(0, 0)
                load_group(1, 1)
                for c in range(GRP):
                    hi_part(0, c, 0)

                yq0 = BASE[f"y{l}"] // 4

                def y_group(jh, par, last):
                    j = jh * 2 + par
                    if last < 2:
                        act.wait_ge(y_lo_done, j * GRP + (W0 + GRP))
                        load_group(j + 2, par)
                    for c in range(GRP):
                        ahead(j * 2 + (yq0 + c // 4), c % 4, last=(l == LAST_L and last == 3 and c == GRP - 1))
                        if last < 3:
                            if c == 0:
                                act.wait_ge(slab_done, j * GRP + BASE[f"y{l}"])
                            hi_part(j + 1, c, 1 - par)

                with act.Fori(0, J // 2 - 1, 1) as jh:
                    y_group(jh, 0, 0)
                    y_group(jh, 1, 0)
                y_group(J // 2 - 1, 0, 2)
                y_group(J // 2 - 1, 1, 3)

            def attention():
                base = BASE["att"]
                q0 = base // 4
                n_norm = [0]

                def after(s):
                    if TILES[s][0] in NORMED:
                        act.wait_ge(hs_taken, n_norm[0] + 1)
                        act.activation(rms_h[:], ms_h[:], ACT.Sqrt).then_inc(rms_h_done, 1)
                        n_norm[0] += 1

                for s in range(20):
                    ahead(q0 + s // 4, s % 4)
                    if TILES[s][0] in NORMED:
                        act.wait_ge(traw_done, sum(k in ROPED for k, _ in TILES[:s]) + 1)
                        act.activation(sqh[s % 2][:].rearrange("p (h t) -> p h t", h=2), acc[:, s % 2, :, 0:HT],
                                       ACT.Square).then_inc(sqh_done, 1)
                    if s:
                        after(s - 1)
                after(19)
                act.wait_ge(rope_done, 20)
                act.dma_start(outs["kT"], kT2[0:HD]).then_inc(kv_out, 16)
                act.dma_start(outs["vT"], vA[:]).then_inc(kv_out, 16)
                act.dma_start(outs["kiT"], kiT[0:HD]).then_inc(kv_out, 16)

                act.wait_ge(prep_done, 2)
                act.activation(v_tok[:, 0:4, :].rearrange("p b (j f) -> p j b f", j=2),
                               misc[:, 0:2, :].rearrange("p j (b f) -> p j b f", b=4), ACT.Copy).then_inc(act_step,
                                                                                                          step.up())
                act.activation(v_tok[0:TS, 4, :], acc[0:TS, 0, 0, 0:2 * P], ACT.Copy).then_inc(prep_taken, 1)

                for i in range(3 * IH):
                    n = (2 + i // IH) * P
                    act.wait_ge(idx_done, i + 1)
                    if i >= 2:
                        act.wait_ge(idx_added, i - 1)
                    act.activation(relu[i % 2][:, 0:n], misc[:, 2 + i % 2, 0:n], ACT.Relu).then_inc(relu_done, 1)
                for u in range(NU + 1):
                    n = UK if u < NU else 1
                    act.wait_ge(unit_used, 4 + TS * (u + 1)) if u < NU else act.wait_ge(s_idx_done, 1)
                    act.activation(relu_s[:, u * UK:u * UK + n], misc[0:HD, 2 + (u % 2), 0:n], ACT.Relu).then_inc(
                        s_relu_done, 1)
                act.wait_ge(s_score_done, NU + 1)
                for u in range(NU + 1):
                    n = UK if u < NU else 1
                    act.wait_ge(unit_used, 4 + TS * (NU + u + 1)) if u < NU else act.wait_ge(s_log_done, 1)
                    act.activation(logits[:, u * UK:u * UK + n], misc[:, 2 + (u % 2), 0:n], ACT.Copy).then_inc(
                        s_log_taken, 1)

                def exp_of(i):
                    b = i // NHEAD
                    n = (b + 1) * P
                    act.wait_ge(nmx_done, i + 1)
                    act.activation(prob[i % 2][:, 0:n], prob[i % 2][:, 0:n], ACT.Exp, bias=nmx[:, i:i + 1],
                                   scale=HD ** -0.5, accum_out=psums[:, i:i + 1]).then_inc(exp_done, 1)

                def take_turned(i):
                    b = i // NHEAD
                    act.wait_ge(ptr_done, i + 1)
                    if i >= 2:
                        act.wait_ge(pv_done, i - 1)
                    act.activation(probT[i % 2][:, 0:b + 1, :], acc[:, 1, i % 2, 0:(b + 1) * P].rearrange(
                        "p (k t) -> p k t", t=P), ACT.Copy).then_inc(pT_done, 1)

                for b in range(4):
                    for h in range(NHEAD + 1):
                        i = b * NHEAD + h
                        if h < NHEAD:
                            exp_of(i)
                        if h:
                            take_turned(i - 1)
                    for k in range(2):
                        act.wait_ge(oT_done, 2 * b + k + 1)
                        act.activation(h_hi[:, 4 * k:4 * k + 4, b * P:(b + 1) * P],
                                       acc[:, 1, k, :].rearrange("p (k t) -> p k t", t=P), ACT.Copy).then_inc(oT_hi, 1)

                act.wait_ge(s_max_done, 1)
                act.activation(logits[:], logits[:], ACT.Exp, bias=smx[:, 1:2], scale=HD ** -0.5,
                               accum_out=smx[:, 2:3]).then_inc(s_exp_done, 1)
                for k in range(NU + 1):
                    act.wait_ge(s_ptr_done, k + 1)
                    if k < NU:
                        act.activation(pT_s[:, 4 * k:4 * k + 4, :], misc[:, 2 + k % 2, :].rearrange(
                            "p (k t) -> p k t", t=P), ACT.Copy).then_inc(s_pT_done, 1)
                    else:
                        act.activation(pnewT[:], misc[0:TS, 2, 0:P], ACT.Copy).then_inc(s_pT_done, 1)
                act.wait_ge(s_pv_done, 1)
                for p in range(2):
                    for kk in range(2):
                        for odd in range(2):
                            src = misc[kk * HD:(kk + 1) * HD, p, 0:HD].rearrange("d (b j) -> d j b", j=8)
                            last = act.activation(oS[odd * HD:(odd + 1) * HD, 4 * p + 2 * kk:4 * p + 2 * kk + 2, :],
                                                  src[:, 4 * kk + odd:4 * kk + odd + 3:2, :], ACT.Copy)
                            last.then_inc(act_step, step.up())
                act.wait_ge(act_step, step.at)
                act.activation(h_hi[:, :, TP:T], oS[:], ACT.Copy).then_inc(oS_done, 1)
                plain("ao")

            peer(0)
            if layers == 2:
                act.wait_ge(acc_free_dve, DVE_TILES["att"] + 2)
                for dst, src in ((cosT, "cos"), (sinT, "sin"), (rot, "rot"), (headones, "headones"), (again, "again"),
                                 (cbias, "cbias"), (sel8, "sel8"), (e64, "e64"), (e8, "e8"), (e8T, "e8T"),
                                 (table, "table")):
                    act.dma_start(dst[:], a[src]).then_inc(att_loaded, 16)
                norm(2, lambda c: (acc_free_dve, DVE_TILES["att"] - 8 + c + 3))
                attention()
                norm(3, lambda c: (acc_free_dve, DVE_TILES["ao"] + c + 3))
                plain("q1")
                peer(1)

        @block.vector
        def _(dve):
            step = Count()
            dve.sem_inc(acc_free_dve, 2)
            dve.sem_inc(acc_free_act, 2)
            dve.sem_inc(gate_taken, 2)
            dve.sem_inc(unit_used, 4)

            def norm(k):
                dve.wait_ge(sumsq_done, k + 1)
                dve.tensor_scalar(ms[:].rearrange("p (h t) -> p h t", h=2), misc[:, 0:2, 0:HT], 1.0 / D, EPS,
                                  ALU.mult, ALU.add).then_inc(ms_done, 1)
                dve.wait_ge(rms_done, k + 1)
                dve.reciprocal(rstd[:], rms[:]).then_inc(rstd_done, 1)
                dve.wait_ge(rstd_done, k + 1)
                for c in range(KC):
                    dve.scalar_tensor_tensor(sq[:, c, :], x[:, c, :], gains[:, k, c:c + 1], rstd[:], ALU.mult,
                                             ALU.mult).then_inc(hf_done, 1)
                for c in range(KC):
                    dve.wait_ge(h_hi_done, k * KC + c + 1)
                    dve.tensor_tensor(h_lo[:, c, :], sq[:, c, :], h_hi[:, c, :].bitcast(F32),
                                      ALU.subtract).then_inc(h_lo_done, 1)

            def halves(t):
                return t.rearrange("p (h t) -> p h t", h=2)

            dve.wait_ge(loaded, 16 * N_CONST)
            dve.tensor_tensor(wsT[:], wsT[:], wcaus[:].unsqueeze(1).to_broadcast([P, GROUPS, P]),
                              ALU.mult).then_inc(dve_step, step.up())
            dve.tensor_tensor(wdiag[:], wdiag[:], weye[:].unsqueeze(1).to_broadcast([TS, GROUPS, TS]),
                              ALU.mult).then_inc(dve_step, step.up())
            norm(0)

            def v_steps(n, first):
                for r in range(4):
                    dve.wait_ge(slab_done, n + r + 1)
                    if not first or r >= 2:
                        dve.wait_ge(vtr_done, n + r - 1)
                    dve.tensor_copy(halves(vT[:, r % 2, :]), acc[:, r % 2, :, 0:HT]).then_inc(acc_free_dve, 1)

            v_steps(0, True)
            with dve.Fori(4, VT, 4) as n:
                v_steps(n, False)

            dve.wait_ge(vss_done, NB)
            dve.tensor_scalar(vms[:, 0:4], vss[:, 0:4], 1.0 / WIDTH, EPS, ALU.mult, ALU.add).then_inc(vms_done, 1)
            dve.tensor_scalar(vms[0:TS, 4:5], vss[0:TS, 4:5], 1.0 / WIDTH, EPS, ALU.mult, ALU.add).then_inc(
                vms_done, 1)
            dve.wait_ge(vrms_done, 2)
            dve.reciprocal(vrstd[:, 0:4], vrms[:, 0:4]).then_inc(vrstd_done, 1)
            dve.reciprocal(vrstd[0:TS, 4:5], vrms[0:TS, 4:5]).then_inc(vrstd_done, 1)
            dve.wait_ge(vrstd_done, 2)
            for b, (t0, w) in enumerate(BLOCK):
                dve.scalar_tensor_tensor(vtok[0:w, b, :], vtok[0:w, b, :], vrstd[0:w, b:b + 1], vgain[0:w, :],
                                         ALU.mult, ALU.mult).then_inc(vnorm_done, 1)

            def mixed(f):
                par, g = f % 2, f // (VT // GROUPS)
                dve.wait_ge(mix_done, f + 1)
                if f >= 2:
                    dve.wait_ge(g_done, f - 1)
                dve.tensor_tensor(mixb[:, par, 0:TP].rearrange("p (b t) -> p b t", b=4),
                                  misc[:, 2 * par, :].rearrange("p (b t) -> p b t", b=4),
                                  mbias[:, g, :].unsqueeze(1).to_broadcast([P, 4, P]), ALU.add).then_inc(mix_added, 1)
                dve.tensor_scalar(mixb[:, par, TP:T], misc[:, 2 * par + 1, 0:TS], mbias[:, g, 0:1], None,
                                  ALU.add).then_inc(mix_added, 1)
                dve.wait_ge(mix_added, 2 * (f + 1))
                dve.tensor_tensor(u[:, f, :], u[:, f, :], mixb[:, par, :], ALU.mult).then_inc(g_done, 1)

            for f in range(VT):
                n = BASE["u_in"] + f
                dve.wait_ge(slab_done, n + 1)
                dve.tensor_copy(halves(u[:, f, :]), acc[:, n % 2, :, 0:HT]).then_inc(acc_free_dve, 1)
                if f >= 4:
                    dve.wait_ge(acc_free_dve, DVE_TILES["u_in"] + f + 1)
                    mixed(f - 4)
            dve.wait_ge(acc_free_dve, DVE_TILES["w_out"] + 2)
            for f in range(VT - 4, VT):
                mixed(f)
            for f in range(VT):
                dve.wait_ge(g_hi_done, f + 1)
                dve.tensor_tensor(g_lo[:, f, :], u[:, f, :], g_hi[:, f, :].bitcast(F32), ALU.subtract).then_inc(
                    g_lo_done, 1)

            for m in range(8):
                dve.wait_ge(slab_done, BASE["w_out"] + 2 * m + 2)
                dve.tensor_tensor(halves(x[:, m, :]), halves(x[:, m, :]), acc[:, m % 2, :, 0:HT], ALU.add).then_inc(
                    acc_free_dve, 1)
            norm(1)

            def q_tiles(l):
                with dve.Fori(0, HTN // 2, 1) as i:
                    for r in range(2):
                        dve.wait_ge(slab_done, i * 2 + (BASE[f"q{l}"] + r + 1))
                        dve.tensor_copy(halves(qT[:, bass.ds(i * 2 + r, 1), :].squeeze(1)),
                                        acc[:, r, :, 0:HT]).then_inc(acc_free_dve, 1)

            def top16(values, scratch, w, best, where, n):
                for k in range(n):
                    dve.max(best(k)[:, 0:8], values(k)).then_inc(dve_step, step.up())
                dve.wait_ge(dve_step, step.at)
                for k in range(n):
                    dve.max_index(where(k)[:, 0:8], best(k)[:, 0:8], values(k)).then_inc(dve_step, step.up())
                    dve.match_replace(scratch(k), best(k)[:, 0:8], values(k), LOW).then_inc(dve_step, step.up())
                dve.wait_ge(dve_step, step.at)
                for k in range(n):
                    dve.max(best(k)[:, 8:16], scratch(k)).then_inc(dve_step, step.up())
                dve.wait_ge(dve_step, step.at)
                for k in range(n):
                    dve.max_index(where(k)[:, 8:16], best(k)[:, 8:16], scratch(k)).then_inc(dve_step, step.up())
                dve.wait_ge(dve_step, step.at)

            def routing(l, b):
                t0, w = BLOCK[b]
                B = l * NB + b
                dve.wait_ge(score_taken, 4 * (B + 1))
                if b or l:
                    dve.wait_ge(routeT_done, B)
                top16(lambda k: sc[0:w, k, :], lambda k: work[0:w, k, :], w, lambda k: keyv[0:w, k, :],
                      lambda k: keyi[0:w, k, :], HTN)
                dve.tensor_copy(keyf[0:w], keyi[0:w]).then_inc(dve_step, step.up())
                kv = keyv[0:w].rearrange("p (h s) k -> p s h k", s=2)
                dve.tensor_tensor(cand[0:w], kv[:, 0].unsqueeze(3).to_broadcast([w, PH, TOPK, TOPK]),
                                  kv[:, 1].unsqueeze(2).to_broadcast([w, PH, TOPK, TOPK]), ALU.add).then_inc(
                    dve_step, step.up())
                dve.wait_ge(dve_step, step.at)
                top16(lambda k: cand[0:w, k].rearrange("p a b -> p (a b)"), lambda k: cwork[0:w, k, :], w,
                      lambda k: topv[0:w, k, :], lambda k: topp[0:w, k, :], PH)
                dve.tensor_tensor(topd[0:w], topv[0:w], topv[0:w, :, 0:1].to_broadcast([w, PH, TOPK]),
                                  ALU.subtract).then_inc(gate_exp_in, 1)
                dve.tensor_scalar(row[0:w, 0], topp[0:w], 4, None, ALU.logical_shift_right).then_inc(dve_step, step.up())
                dve.tensor_scalar(row[0:w, 1], topp[0:w], 15, None, ALU.bitwise_and).then_inc(dve_step, step.up())
                dve.wait_ge(dve_step, step.at)
                dve.tensor_copy(rowf[0:w], row[0:w]).then_inc(dve_step, step.up())
                dve.wait_ge(dve_step, step.at)
                kf = keyf[0:w].rearrange("p (h s) k -> p s h k", s=2)
                for s in range(2):
                    dve.tensor_tensor(hot[0:w].rearrange("p h k a -> p (h k) a"),
                                      rowf[0:w, s].rearrange("p h k -> p (h k)").unsqueeze(2).to_broadcast(
                                          [w, SLOTS, TOPK]),
                                      iota[0:w, 0:TOPK].unsqueeze(1).to_broadcast([w, SLOTS, TOPK]),
                                      ALU.is_equal).then_inc(dve_step, step.up())
                    dve.wait_ge(dve_step, step.at)
                    dve.tensor_tensor(hot[0:w], hot[0:w], kf[:, s].unsqueeze(2).to_broadcast([w, PH, TOPK, TOPK]),
                                      ALU.mult).then_inc(dve_step, step.up())
                    dve.wait_ge(dve_step, step.at)
                    dve.tensor_reduce(route[0:w, s], hot[0:w], AX, ALU.add).then_inc(dve_step, step.up())
                    dve.wait_ge(dve_step, step.at)
                dve.wait_ge(gate_exp_done, B + 1)
                dve.tensor_reduce(gsum[0:w, 0], route[0:w, 2], AX, ALU.add).then_inc(dve_step, step.up())
                dve.wait_ge(dve_step, step.at)
                dve.reciprocal(gsum[0:w, 1], gsum[0:w, 0]).then_inc(dve_step, step.up())
                dve.wait_ge(dve_step, step.at)
                dve.tensor_tensor(route[0:w, 2], route[0:w, 2],
                                  gsum[0:w, 1].unsqueeze(2).to_broadcast([w, PH, TOPK]), ALU.mult).then_inc(
                    route_done, 1)

            def one_hots(half, t0, par, first):
                if not first:
                    dve.wait_ge(gate_mm, half * 2 - 2)
                    dve.wait_ge(hg_lo_done, half - 1)
                shape = [P, HG, P]
                key = iota[:].unsqueeze(1).to_broadcast(shape)
                dve.tensor_tensor(hot1[par][:], idxT[:, 0, bass.ds(t0, HG)].unsqueeze(2).to_broadcast(shape), key,
                                  ALU.is_equal)
                dve.tensor_tensor(hot2[par][:], idxT[:, 1, bass.ds(t0, HG)].unsqueeze(2).to_broadcast(shape), key,
                                  ALU.is_equal).then_inc(hot2_done, 1)
                dve.wait_ge(hot2_done, half + 1)
                dve.tensor_tensor(hg_hi[par][:], hot2[par][:],
                                  gate_hi[:, bass.ds(t0, HG)].bitcast(F32).unsqueeze(2).to_broadcast(shape),
                                  ALU.mult).then_inc(hot_done, 1)

            def peer(l):
                if l:
                    dve.wait_ge(kv_out, 48)
                q_tiles(l)
                H0 = l * (2 * NG - 1)
                for b, (t0, w) in enumerate(BLOCK):
                    B = l * NB + b
                    routing(l, b)
                    dve.wait_ge(slotT_done, B + 1)
                    dve.tensor_tensor(gate_lo[:, t0:t0 + w], gateT[:, t0:t0 + w], gate_hi[:, t0:t0 + w].bitcast(F32),
                                      ALU.subtract).then_inc(gate_lo_done, 1)
                    if b < 4:
                        hb = H0 + t0 // HG
                        lead = 1 if hb == 0 else 0
                        if lead:
                            for par in range(2):
                                one_hots(hb + par, t0 + par * HG, par, True)
                        with dve.Fori(lead, P // TG, 1) as i:
                            for par in range(2):
                                one_hots(i * 2 + (hb + par), i * TG + (t0 + par * HG), par, False)
                    else:
                        one_hots(H0 + TP // HG, TP, 0, False)

                for par in range(2):
                    dve.wait_ge(act_stored[par], (l + 1) * (NK // 2) * 16)
                dve.wait_ge(gate_stored[0], (l + 1) * ((NG + 1) // 2) * 16)
                dve.wait_ge(gate_stored[1], (l + 1) * (NG // 2) * 16)
                dve.memset(abuf[0][:, :, T:TW], 0.0).then_inc(dve_step, step.up())
                dve.memset(abuf[1][:, :, T:TW], 0.0).then_inc(dve_step, step.up())
                dve.wait_ge(dve_step, step.at)
                dve.sem_inc(pad_done, 1)

                W0 = l * NK
                J = NK // GRP
                GL0 = l * (J // 2)

                def weigh(j, jh, c, par):
                    if c == 0:
                        dve.wait_ge(group_loaded[par], jh * 32 + 32 * (GL0 + 1))
                    dve.tensor_tensor(abuf[par][:, c, :].rearrange("p (n t) -> p n t", t=TG),
                                      abuf[par][:, c, :].rearrange("p (n t) -> p n t", t=TG),
                                      gbuf[par][:, :, c, :], ALU.mult).then_inc(y_mult, 1)

                for c in range(GRP):
                    weigh(0, 0, c, 0)

                def y_group(jh, par, last):
                    for c in range(GRP):
                        j = jh * 2 + par
                        if not last:
                            weigh(j + 1, jh + par, c, 1 - par)
                        dve.wait_ge(slab_done, j * GRP + (BASE[f"y{l}"] + c + 1))
                        dve.wait_ge(acc_free_dve, j * GRP + (DVE_TILES[f"y{l}"] + c + 2 - GRP + 1))
                        dve.tensor_tensor(halves(x[:, c, :]), halves(x[:, c, :]), acc[:, c % 2, :, 0:HT],
                                          ALU.add).then_inc(acc_free_dve, 1)

                with dve.Fori(0, J // 2 - 1, 1) as jh:
                    y_group(jh, 0, False)
                    y_group(jh, 1, False)
                y_group(J // 2 - 1, 0, False)
                y_group(J // 2 - 1, 1, True)

            def attention():
                base = BASE["att"]
                n_norm, n_rot = [0], [0]
                dve.wait_ge(att_loaded, 16 * N_ATT)
                dve.wait_ge(h_lo_done, 3 * KC)
                dve.memset(qiM[:], 0.0).then_inc(dve_step, step.up())
                dve.memset(qM[:], 0.0).then_inc(dve_step, step.up())
                dve.wait_ge(dve_step, step.at)
                dve.sem_inc(sel_ready, 1)
                dest = {"ki": lambda j: kiT[:], "wi": lambda j: wiT[:], "qi": lambda j: qiT[:, j, :],
                        "k": lambda j: kT2[:, j, :], "v": lambda j: vA[:, j, :], "q": lambda j: qA[:, j, :]}

                def after(s):
                    kind, j = TILES[s]
                    par = s % 2
                    if kind not in ROPED:
                        return
                    if s:
                        dve.wait_ge(rope_done, s)
                    dve.tensor_tensor(ra[:], traw[par][:], cosT[:], ALU.mult).then_inc(dve_step, step.up())
                    if kind in NORMED:
                        dve.wait_ge(hs_done, n_norm[0] + 1)
                        dve.tensor_scalar(halves(ms_h[:]), misc[:, 0:2, 0:HT], 1.0 / HD, EPS, ALU.mult,
                                          ALU.add).then_inc(hs_taken, 1)
                        n_norm[0] += 1
                    dve.wait_ge(rot_done, n_rot[0] + 1)
                    n_rot[0] += 1
                    dve.tensor_tensor(halves(rb[:]), acc[:, par, :, 0:HT], halves(sinT[:]), ALU.mult).then_inc(
                        acc_free_dve, 1)
                    dve.wait_ge(acc_free_dve, DVE_TILES["att"] + s + 3)
                    dve.wait_ge(dve_step, step.at)
                    if kind in NORMED:
                        dve.tensor_tensor(ra[:], ra[:], rb[:], ALU.add).then_inc(dve_step, step.up())
                        dve.wait_ge(rms_h_done, n_norm[0])
                        dve.reciprocal(rms_h[:], rms_h[:]).then_inc(dve_step, step.up())
                        dve.wait_ge(dve_step, step.at)
                        dve.tensor_tensor(dest[kind](j), ra[:], rms_h[:], ALU.mult).then_inc(rope_done, 1)
                    else:
                        dve.tensor_tensor(dest[kind](j), ra[:], rb[:], ALU.add).then_inc(rope_done, 1)

                for s in range(20):
                    kind, j = TILES[s]
                    par = s % 2
                    dve.wait_ge(slab_done, base + s + 1)
                    src = acc[:, par, :, 0:HT]
                    if kind in NORMED:
                        g = NORMED[kind]
                        dve.tensor_scalar(halves(traw[par][:]), src, again[:, g:g + 1], None, ALU.mult).then_inc(
                            traw_done, 1)
                        dve.wait_ge(traw_done, n_traw[0] + 1)
                        n_traw[0] += 1
                    elif kind in ROPED:
                        dve.tensor_copy(halves(traw[par][:]), src).then_inc(traw_done, 1)
                        dve.wait_ge(traw_done, n_traw[0] + 1)
                        n_traw[0] += 1
                    if s:
                        after(s - 1)
                    if kind not in ROPED:
                        dve.tensor_copy(halves(dest[kind](j)), src).then_inc(acc_free_dve, 1)
                        dve.wait_ge(acc_free_dve, DVE_TILES["att"] + s + 3)
                        dve.sem_inc(rope_done, 1)
                after(19)
                dve.wait_ge(rope_done, 20)

                def diag(t, width):
                    return t.rearrange("p (b w) -> p b w", w=width)

                qi_rows = diag(qiM[:], HD + 8)
                for odd in range(2):
                    dve.tensor_copy(qi_rows[:, :, odd:8:2], qiT[odd * HD:(odd + 1) * HD, :, TP:T].rearrange(
                        "d i b -> d b i")).then_inc(dve_step, step.up())
                for h in range(NHEAD):
                    p, kk, odd = h // 8, h // 4 % 2, h % 2
                    dve.tensor_copy(diag(qM[:, p, :], P + 16)[kk * HD:(kk + 1) * HD, :, h],
                                    qA[odd * HD:(odd + 1) * HD, h // 2, TP:T]).then_inc(dve_step, step.up())
                for p in range(2):
                    for kk in range(2):
                        dve.tensor_copy(knew[kk * HD:(kk + 1) * HD, p, :],
                                        kT2[kk * HD:(kk + 1) * HD, 2 * p + kk, TP:T]).then_inc(dve_step, step.up())
                dve.wait_ge(dve_step, step.at)
                dve.sem_inc(qM_ready, 1)
                dve.wait_ge(prep_done, 1)
                dve.tensor_scalar(wi_tok[:].rearrange("p b h -> p (b h)"), misc[:, 2, 0:4 * IH], IDX_SCALE, None,
                                  ALU.mult).then_inc(dve_step, step.up())
                dve.scalar_tensor_tensor(wiB[:], misc[0:HD, 3, 0:TS], IDX_SCALE, e64[:], ALU.mult, ALU.mult).then_inc(
                    dve_step, step.up())
                dve.wait_ge(dve_step, step.at)
                dve.sem_inc(prep_taken, 1)

                for i in range(3 * IH):
                    b, h = 1 + i // IH, i % IH
                    n = (b + 1) * P
                    dve.wait_ge(relu_done, i + 1)
                    if h:
                        dve.wait_ge(idx_added, i)
                        dve.scalar_tensor_tensor(idxs[:, b, 0:n], relu[i % 2][:, 0:n], wi_tok[:, b, h:h + 1],
                                                 idxs[:, b, 0:n], ALU.mult, ALU.add).then_inc(idx_added, 1)
                    else:
                        dve.tensor_scalar(idxs[:, b, 0:n], relu[i % 2][:, 0:n], wi_tok[:, b, h:h + 1], None,
                                          ALU.mult).then_inc(idx_added, 1)
                dve.wait_ge(idx_added, 3 * IH)
                for b in range(1, 4):
                    diagonal = idxs[:, b, b * P:(b + 1) * P]
                    dve.tensor_tensor(diagonal, diagonal, cbias[:], ALU.add).then_inc(dve_step, step.up())
                dve.wait_ge(dve_step, step.at)
                for _ in range(KEEP_P // 8):
                    for b in range(1, 4):
                        dve.max(m8[:, b - 1, :], idxs[:, b, 0:(b + 1) * P]).then_inc(dve_step, step.up())
                    dve.wait_ge(dve_step, step.at)
                    for b in range(1, 4):
                        keys = idxs[:, b, 0:(b + 1) * P]
                        dve.match_replace(keys, m8[:, b - 1, :], keys, LOW).then_inc(dve_step, step.up())
                    dve.wait_ge(dve_step, step.at)
                for b in range(1, 4):
                    keys = idxs[:, b, 0:(b + 1) * P]
                    dve.tensor_scalar(keys, keys, LOW, OUT, ALU.not_equal, ALU.mult).then_inc(dve_step, step.up())
                dve.tensor_copy(idxs[:, 0, 0:P], cbias[:]).then_inc(dve_step, step.up())
                dve.wait_ge(dve_step, step.at)

                for u in range(NU + 1):
                    n = UK if u < NU else 1
                    dve.wait_ge(s_score_done, u + 1)
                    dve.tensor_copy(score8[:, u * UK:u * UK + n], misc[0:TS, 2 + u % 2, 0:n]).then_inc(s_score_taken, 1)

                def biased(i):
                    b = i // NHEAD
                    n = (b + 1) * P
                    dve.wait_ge(log_done, i + 1)
                    if i >= 2:
                        dve.wait_ge(ptr_done, i - 1)
                    dve.tensor_tensor_reduce(out=prob[i % 2][:, 0:n], in0=acc[:, 0, i % 2, 0:n], in1=idxs[:, b, 0:n],
                                             scale=1.0, scalar=LOW, op0=ALU.add, op1=ALU.max,
                                             accum_out=mx[:, i:i + 1]).then_inc(log_taken, 1)
                    dve.wait_ge(log_taken, i + 1)
                    dve.tensor_scalar(nmx[:, i:i + 1], mx[:, i:i + 1], -(HD ** -0.5), None, ALU.mult).then_inc(
                        nmx_done, 1)

                def output(i):
                    h = i % NHEAD
                    dve.wait_ge(exp_done, i + 1)
                    dve.reciprocal(rinv[:, i:i + 1], psums[:, i:i + 1]).then_inc(dve_step, step.up())
                    dve.wait_ge(dve_step, step.at)
                    dve.wait_ge(pv_done, i + 1)
                    dve.tensor_scalar(o_tok[:, h * HD:(h + 1) * HD], misc[:, i % 2, 0:HD],
                                      rinv[:, i:i + 1], None, ALU.mult).then_inc(o_done, 1)

                for b in range(4):
                    for h in range(NHEAD + 2):
                        i = b * NHEAD + h
                        if h < NHEAD:
                            biased(i)
                        if h >= 2:
                            if h == 2 and b:
                                dve.wait_ge(oT_done, 2 * b)
                            output(i - 2)
                    for k in range(2):
                        dve.wait_ge(oT_hi, 2 * b + k + 1)
                        part = h_hi[:, 4 * k:4 * k + 4, b * P:(b + 1) * P]
                        dve.tensor_tensor(h_lo[:, 4 * k:4 * k + 4, b * P:(b + 1) * P],
                                          acc[:, 1, k, :].rearrange("p (k t) -> p k t", t=P), part.bitcast(F32),
                                          ALU.subtract).then_inc(oT_lo, 1)

                dve.wait_ge(s_score_taken, NU + 1)
                for k in range(KEEP_S // 8):
                    dve.max(m8[0:TS, 0, :], score8[:]).then_inc(s_top, 1)
                    dve.wait_ge(s_top, k * 2 + 1)
                    dve.match_replace(score8[:], m8[0:TS, 0, :], score8[:], LOW).then_inc(s_top, 1)
                    dve.wait_ge(s_top, k * 2 + 2)
                dve.tensor_scalar(score8[:], score8[:], LOW, OUT, ALU.not_equal, ALU.mult).then_inc(mask_ready, 1)
                for u in range(NU + 1):
                    n = UK if u < NU else 1
                    dve.wait_ge(bias_done, u + 1)
                    part = logits[:, u * UK:u * UK + n]
                    if u == 0:
                        dve.wait_ge(s_log_taken, NU + 1)
                    dve.tensor_tensor(part, part, misc[:, 2 + u % 2, 0:n], ALU.add).then_inc(bias_taken, 1)
                dve.wait_ge(bias_taken, NU + 1)
                dve.tensor_reduce(smx[:, 0:1], logits[:], AX, ALU.max).then_inc(dve_step, step.up())
                dve.wait_ge(dve_step, step.at)
                dve.tensor_scalar(smx[:, 1:2], smx[:, 0:1], -(HD ** -0.5), None, ALU.mult).then_inc(s_max_done, 1)
                dve.wait_ge(s_exp_done, 1)
                dve.reciprocal(smx[:, 3:4], smx[:, 2:3]).then_inc(dve_step, step.up())
                dve.wait_ge(dve_step, step.at)
                dve.tensor_scalar(logits[:], logits[:], smx[:, 3:4], None, ALU.mult).then_inc(s_prob_done, 1)
                dve.wait_ge(s_prob_done, 1)
                dve.tensor_scalar(pnew[:], e8[:], logits[:, PAST:SK], None, ALU.mult).then_inc(s_prob_done, 1)
                dve.wait_ge(oS_done, 1)
                dve.tensor_tensor(h_lo[:, :, TP:T], oS[:], h_hi[:, :, TP:T].bitcast(F32), ALU.subtract).then_inc(
                    oS_done, 1)

                for m in range(8):
                    dve.wait_ge(slab_done, BASE["ao"] + m + 1)
                    dve.tensor_tensor(halves(x[:, m, :]), halves(x[:, m, :]), acc[:, m % 2, :, 0:HT], ALU.add).then_inc(
                        acc_free_dve, 1)
                dve.wait_ge(acc_free_dve, DVE_TILES["ao"] + 8 + 2)

            n_traw = [0]
            peer(0)
            if layers == 2:
                dve.wait_ge(acc_free_dve, DVE_TILES["att"] + 2)
                norm(2)
                attention()
                norm(3)
                peer(1)

        @block.gpsimd
        def _(pool):
            def split(q, r, first=False):
                pool.wait_ge(hi_done, q * 4 + (r + 1))
                if not first:
                    pool.wait_ge(slab_done, q * 4 + (r - 1))
                pool.tensor_tensor(w_lo[r % 2][:], raw[r][:], w_hi[r % 2][:].bitcast(F32), ALU.subtract).then_inc(
                    lo_done, 1)

            def ahead(q, r, last=False):
                if not last:
                    split(q + 1 if r == 3 else q, (r + 1) % 4)

            def plain(q0, count):
                with pool.Fori(q0, q0 + count, 1) as q:
                    for r in range(4):
                        ahead(q, r)

            split(0, 0, first=True)
            plain(0, BASE["s0"] // 4)

            def peer(l):
                q0 = BASE[f"s{l}"] // 4
                done = 0
                H0 = l * (2 * NG - 1)

                def gate_low(half, t0, par, first=False):
                    shape = [P, HG, P]
                    pool.wait_ge(hot2_done, half + 1)
                    if not first:
                        pool.wait_ge(gate_mm, half * 2 - 2)
                    pool.tensor_tensor(hg_lo[par][:], hot2[par][:],
                                       gate_lo[:, bass.ds(t0, HG)].unsqueeze(2).to_broadcast(shape),
                                       ALU.mult).then_inc(hg_lo_done, 1)

                for b, (t0, w) in enumerate(BLOCK):
                    B = l * NB + b
                    plain(q0 + done // 4, 4)
                    done += 16
                    pool.wait_ge(gate_lo_done, B + 1)
                    if b < 4:
                        def steps(i, first):
                            for r in range(4):
                                ahead(i + (q0 + done // 4), r)
                                for par in range(2):
                                    half = i * 8 + (H0 + t0 // HG + 2 * r + par)
                                    gate_low(half, i * 8 * HG + (t0 + (2 * r + par) * HG), par, first and r == 0)
                        if B == 0:
                            steps(0, True)
                            steps(1, False)
                        else:
                            with pool.Fori(0, 2, 1) as i:
                                steps(i, False)
                        done += 8
                    else:
                        gate_low(H0 + TP // HG, TP, 0)
                plain(q0 + done // 4, (NK - done) // 4)

                W0 = l * NK
                J = NK // GRP

                def low_part(j, c, par):
                    pool.wait_ge(y_hi_done, j * GRP + (W0 + c + 1))
                    pool.tensor_tensor(y_lo[par][:, c, :], abuf[par][:, c, 0:T], y_hi[par][:, c, :].bitcast(F32),
                                       ALU.subtract).then_inc(y_lo_done, 1)

                for c in range(GRP):
                    low_part(0, c, 0)
                yq0 = BASE[f"y{l}"] // 4

                def y_group(j, par, last):
                    for c in range(GRP):
                        ahead(j * 2 + (yq0 + c // 4), c % 4, last=l == LAST_L and last and c == GRP - 1)
                        if not last:
                            low_part(j + 1, c, 1 - par)

                with pool.Fori(0, J - 2, 2) as j:
                    y_group(j, 0, False)
                    y_group(j + 1, 1, False)
                y_group(J - 2, 0, False)
                y_group(J - 1, 1, True)

            peer(0)
            if layers == 2:
                plain(BASE["att"] // 4, (BASE["s1"] - BASE["att"]) // 4)
                peer(1)
                pool.wait_ge(kv_out, 48)
            pool.wait_ge(acc_free_dve, DVE_TILES[f"y{LAST_L}"] + NK + 2)
            pool.dma_start(outs["yT"], x[:]).then_inc(stored, 16)
            pool.wait_ge(stored, 16)
            pool.wait_ge(vout, 16)


def _slabs(w):
    n = w.shape[1] // P
    return w.reshape(KC, P, n, P).transpose(2, 1, 0, 3).reshape(n, P, D)


def att_slabs(i):
    w = np.asarray(i["att_w_in"])[0]
    q, k, v, qi, ki, wi = np.split(w, np.cumsum([NHEAD * HD, NKV * HD, NKV * HD, IH * HD, HD]), axis=1)
    twice = np.concatenate([k[:, j // 2 * HD:(j // 2 + 1) * HD] for j in range(2 * NKV)], 1)
    pad = np.concatenate([wi, np.zeros((D, P - IH), np.float32)], 1)
    return [_slabs(np.concatenate([ki, ki, pad, qi, twice, v, q], 1)), _slabs(np.asarray(i["att_w_out"])[0])]


def rotary():
    f = np.float32
    half = HD // 2
    inv = np.exp(f(-math.log(10000.0)) * np.arange(half, dtype=f) / f(half)).astype(f)
    pos = np.concatenate([np.arange(TP), np.full(TS, PAST)]).astype(f)
    ang = (pos[None, :] * inv[:, None]).astype(f)
    swap = np.zeros((P, P), f)
    for m in range(P):
        swap[m ^ half, m] = -1.0 if m % HD < half else 1.0
    return np.tile(np.cos(ang), (4, 1)).astype(f), np.tile(np.sin(ang), (4, 1)).astype(f), swap


def layout(i, layers=2):
    w_in = np.asarray(i["gmlp_w_in"])[0]
    f = np.float32
    slabs = [_slabs(w_in[:, WIDTH:]), _slabs(w_in[:, :WIDTH]),
             np.asarray(i["gmlp_w_out"])[0].reshape(2, KC, P, 8, P).transpose(3, 0, 2, 1, 4).reshape(16, P, D)]
    for l in range(layers):
        if l == 1:
            slabs += att_slabs(i)
        slabs.append(_slabs(np.asarray(i["peer_w_q"])[l]))
        slabs.append(np.asarray(i["peer_u"])[l].reshape(P, NK, KC, P).transpose(1, 3, 2, 0).reshape(NK, P, D))
        slabs.append(np.asarray(i["peer_v"])[l].reshape(P, NK // GRP, GRP, KC, P).transpose(1, 3, 0, 2, 4).reshape(
            NK, P, D))
    xs = np.concatenate([np.asarray(i["x_prompt"])[0], np.asarray(i["x_sample"])[:, 0]], 0)
    ws = np.asarray(i["gmlp_w_s"])[0]
    keys = np.stack([np.asarray(i[n])[l].T for l in range(2) for n in ("peer_sub_k1", "peer_sub_k2")], 1)
    gains = np.stack([np.asarray(i[n])[l].reshape(KC, P).T for l in range(2) for n in ("norm_mix_g", "norm_ffn_g")], 1)
    s, t = np.arange(P)[:, None], np.arange(P)[None, :]
    arrays = {
        "slabs": np.concatenate(slabs, 0),
        "xT": xs.T.reshape(KC, P, T).transpose(1, 0, 2),
        "ident": np.eye(P, dtype=f),
        "ones": np.ones((P, P), f),
        "gains": gains,
        "iota": np.broadcast_to(np.arange(P, dtype=f), (P, P)),
        "vgain": np.asarray(i["gmlp_v_g"])[0],
        "mbias": np.asarray(i["gmlp_b_s"])[0].reshape(-1),
        "wsT": ws.transpose(2, 0, 1),
        "wdiag": np.broadcast_to(ws[:, 0, 0][None, :, None], (TS, GROUPS, TS)),
        "wcaus": (s <= t).astype(f),
        "weye": np.eye(TS, dtype=f),
        "subk": keys,
    }
    if layers == 2:
        cos, sin, swap = rotary()
        g = np.stack([np.tile(np.asarray(i[n])[0], 2) for n in ("att_q_norm_g", "att_k_norm_g", "att_idx_k_norm_g")], 1)
        ck = np.asarray(i["cache_k"])[0]
        own = np.arange(P)[:, None] // 16 == np.arange(TS)[None, :]
        arrays |= {
            "cos": cos, "sin": sin, "rot": swap,
            "headones": np.kron(np.eye(2, dtype=f), np.ones((HD, HD), f)),
            "again": g,
            "cbias": np.where(t <= s, f(0), f(OUT)).astype(f),
            "sel8": np.tile(np.eye(IH, dtype=f), (1, TS)),
            "e64": np.kron(np.eye(TS, dtype=f), np.ones((IH, 1), f)),
            "e8": own.astype(f), "e8T": own.T.astype(f),
            "table": np.asarray(i["page_table"]).reshape(1, -1),
            "ckT": ck.reshape(NPOOL, P, 2, P).transpose(0, 3, 2, 1),
            "cv": np.asarray(i["cache_v"])[0].reshape(NPOOL, P, NKV * HD),
            "cikT": np.asarray(i["cache_idx_k"])[0].transpose(0, 2, 1),
        }
    return {k: np.ascontiguousarray(v) for k, v in arrays.items()}


def kernel(**inputs):
    import concourse.bacc as bacc
    from concourse.bass_utils import run_bass_kernel_spmd

    arrays = layout(inputs)
    nc = bacc.Bacc("TRN2", target_bir_lowering=False, num_devices=1)
    a = {n: nc.dram_tensor(f"{n}_in", v.shape, mybir.dt.from_np(v.dtype), kind="ExternalInput").ap()
         for n, v in arrays.items()}
    outs = {n: nc.dram_tensor(f"{n}_out", s, F32, kind="ExternalOutput").ap() for n, s in OUTS.items()}
    build(nc, a, outs)
    r = run_bass_kernel_spmd(nc, [{f"{n}_in": v for n, v in arrays.items()}], core_ids=[0]).results[0]
    y = r["yT_out"].transpose(1, 0, 2).reshape(D, T).T
    k = r["kT_out"].transpose(2, 1, 0)
    v = r["vT_out"].transpose(1, 0, 2).reshape(NKV * HD, T).T.reshape(T, NKV, HD)
    ki = r["kiT_out"].T
    return (y[None, :TP], y[TP:, None], k[None, None, :TP], v[None, None, :TP], ki[None, None, :TP],
            k[None, TP:, None], v[None, TP:, None], ki[None, TP:, None], r["chunk_v_out"][None, :, None])
```
